# Optimizing a Trainium2 kernel written in Bass

```python
import jax, jax.numpy as jnp
from jax import lax
import numpy as np

D_MODEL = 1024
BATCH = 1
SEQ = 256
DEPTH = 2

GRID_W = 64
CTX_LEN = 256

HEAD_DIM = 64
A_HEADS = 8
A_KV_HEADS = 2
A_GROUP = A_HEADS // A_KV_HEADS
A_WINDOW = 128
BLOCK = 128
B_CH = 256
B_WIDTH = 31
C_HEADS = 4
C_Q_RANK = 384
C_KV_RANK = 256
C_NOPE = 64
C_ROPE = 32
C_V = 64

A_Q = A_HEADS * HEAD_DIM
A_KV = A_KV_HEADS * HEAD_DIM
MIX_WIDTH = A_Q + B_CH + C_HEADS * C_V
IN_SPLITS = (A_Q, A_Q + A_KV, A_Q + 2 * A_KV, A_Q + 2 * A_KV + 2 * B_CH,
             A_Q + 2 * A_KV + 2 * B_CH + C_Q_RANK, A_Q + 2 * A_KV + 2 * B_CH + C_Q_RANK + C_KV_RANK)
IN_COLS = IN_SPLITS[-1] + C_ROPE

D_FF = ((8 * D_MODEL // 3 + 127) // 128) * 128
N_EXPERTS = 8
TOP_K = 2

ROPE_BASE = 10000.0
EPS = 1e-6
NEG = -1e30
A_SCALE = HEAD_DIM ** -0.5
MLA_SCALE = (C_NOPE + C_ROPE) ** -0.5

kernel_name = "hybrid_parallel_heads_dit_block"

def rms_norm(x, g):
    xf = x.astype(jnp.float32)
    y = xf * lax.rsqrt(jnp.mean(xf * xf, axis=-1, keepdims=True) + EPS)
    return y.astype(x.dtype) * g

def layer_norm(x, g, b):
    xf = x.astype(jnp.float32)
    mu = jnp.mean(xf, axis=-1, keepdims=True)
    var = jnp.mean(jnp.square(xf - mu), axis=-1, keepdims=True)
    return ((xf - mu) * lax.rsqrt(var + EPS)).astype(x.dtype) * g + b

def modulate(h, shift, scale):
    return h * (1 + scale) + shift

def axial_tables(rows, cols, rot_dim, dtype):
    a = rot_dim // 2
    inv = 1.0 / (ROPE_BASE ** (jnp.arange(0, a, 2, dtype=jnp.float32) / a))
    ar = rows.astype(jnp.float32)[:, None] * inv
    ac = cols.astype(jnp.float32)[:, None] * inv
    return (jnp.cos(ar).astype(dtype), jnp.sin(ar).astype(dtype),
            jnp.cos(ac).astype(dtype), jnp.sin(ac).astype(dtype))

def rope_half(x, cos, sin):
    d2 = x.shape[-1] // 2
    x1, x2 = x[..., :d2], x[..., d2:]
    cs, sn = cos[:, None, :], sin[:, None, :]
    return jnp.concatenate([x1 * cs - x2 * sn, x1 * sn + x2 * cs], axis=-1)

def rope_2d(x, tab):
    cr, sr, cc, sc = tab
    a = x.shape[-1] // 2
    return jnp.concatenate([rope_half(x[..., :a], cr, sr), rope_half(x[..., a:], cc, sc)], axis=-1)

def softmax_with_sink(s, sink):
    m = jnp.maximum(jnp.max(s, axis=-1, keepdims=True), sink)
    e = jnp.exp(s - m)
    return e / (jnp.sum(e, axis=-1, keepdims=True) + jnp.exp(sink - m))

def mixer_inputs(p, a_qg, a_kg, c_qrank_g, c_kvrank_g, w_uq, w_ukv, c_qn_g, c_kn_g, c_qr_g, c_kr_g):
    bsz, n = p.shape[:2]
    qa, ka, va, ub, cq, ckv, kr = jnp.split(p, IN_SPLITS, axis=-1)
    qa = rms_norm(qa.reshape(bsz, n, A_HEADS, HEAD_DIM), a_qg)
    ka = rms_norm(ka.reshape(bsz, n, A_KV_HEADS, HEAD_DIM), a_kg)
    va = va.reshape(bsz, n, A_KV_HEADS, HEAD_DIM)
    q_c = (rms_norm(cq, c_qrank_g) @ w_uq).reshape(bsz, n, C_HEADS, C_NOPE + C_ROPE)
    kv_c = (rms_norm(ckv, c_kvrank_g) @ w_ukv).reshape(bsz, n, C_HEADS, C_NOPE + C_V)
    qn = rms_norm(q_c[..., :C_NOPE], c_qn_g)
    qr = rms_norm(q_c[..., C_NOPE:], c_qr_g)
    kn = rms_norm(kv_c[..., :C_NOPE], c_kn_g)
    vc = kv_c[..., C_NOPE:]
    kr = rms_norm(kr, c_kr_g)
    return qa, ka, va, ub, qn, qr, kn, kr, vc

def window_attention(q, k, v, k_ctx, v_ctx, sink):
    bsz, t = q.shape[:2]
    qg = q.reshape(bsz, t, A_KV_HEADS, A_GROUP, HEAD_DIM)
    pad = ((0, 0), (BLOCK, BLOCK), (0, 0), (0, 0))
    kp, vp = jnp.pad(k, pad), jnp.pad(v, pad)
    sink_b = sink.astype(jnp.float32).reshape(A_KV_HEADS, A_GROUP)[None, :, :, None, None]

    def block(n):
        st = n * BLOCK
        qb = lax.dynamic_slice_in_dim(qg, st, BLOCK, axis=1)
        kb = lax.dynamic_slice_in_dim(kp, st, 3 * BLOCK, axis=1)
        vb = lax.dynamic_slice_in_dim(vp, st, 3 * BLOCK, axis=1)
        s_loc = jnp.einsum('bqhgd,bkhd->bhgqk', qb, kb).astype(jnp.float32) * A_SCALE
        qpos = st + jnp.arange(BLOCK)
        kpos = st - BLOCK + jnp.arange(3 * BLOCK)
        valid = ((kpos[None, :] >= 0) & (kpos[None, :] < t)
                 & (jnp.abs(qpos[:, None] - kpos[None, :]) <= A_WINDOW))
        s_loc = jnp.where(valid, s_loc, NEG)
        s_ctx = jnp.einsum('bqhgd,blhd->bhgql', qb, k_ctx).astype(jnp.float32) * A_SCALE
        p = softmax_with_sink(jnp.concatenate([s_loc, s_ctx], axis=-1), sink_b).astype(v.dtype)
        return (jnp.einsum('bhgqk,bkhd->bqhgd', p[..., :3 * BLOCK], vb)
                + jnp.einsum('bhgql,blhd->bqhgd', p[..., 3 * BLOCK:], v_ctx))

    o = lax.map(block, jnp.arange(t // BLOCK))
    return o.transpose(1, 0, 2, 3, 4, 5).reshape(bsz, t, A_Q)

def ctx_gqa(q, k, v, sink):
    bsz, n = q.shape[:2]
    qg = q.reshape(bsz, n, A_KV_HEADS, A_GROUP, HEAD_DIM)
    sink_b = sink.astype(jnp.float32).reshape(A_KV_HEADS, A_GROUP)[None, :, :, None, None]
    s = jnp.einsum('bqhgd,bkhd->bhgqk', qg, k).astype(jnp.float32) * A_SCALE
    p = softmax_with_sink(s, sink_b).astype(v.dtype)
    return jnp.einsum('bhgqk,bkhd->bqhgd', p, v).reshape(bsz, n, A_Q)

def conv_module(u2, w, b, ln_g, ln_b):
    a, g = jnp.split(u2, 2, axis=-1)
    u = a * jax.nn.sigmoid(g)
    y = lax.conv_general_dilated(u, w[:, None, :].astype(u.dtype), (1,), [(B_WIDTH // 2, B_WIDTH // 2)],
                                 dimension_numbers=('NWC', 'WIO', 'NWC'), feature_group_count=B_CH) + b
    return jax.nn.silu(layer_norm(y, ln_g, ln_b))

def mla_core(qn, qr, kn, kr, v):
    s = (jnp.einsum('bqhd,bkhd->bhqk', qn, kn)
         + jnp.einsum('bqhd,bkd->bhqk', qr, kr)).astype(jnp.float32) * MLA_SCALE
    p = jax.nn.softmax(s, axis=-1).astype(v.dtype)
    o = jnp.einsum('bhqk,bkhd->bqhd', p, v)
    return o.reshape(o.shape[0], o.shape[1], C_HEADS * C_V)

def mla_blocks(qn, qr, kn, kr, v):
    bsz, t = qn.shape[:2]

    def block(n):
        st = n * BLOCK
        return mla_core(lax.dynamic_slice_in_dim(qn, st, BLOCK, axis=1),
                        lax.dynamic_slice_in_dim(qr, st, BLOCK, axis=1), kn, kr, v)

    o = lax.map(block, jnp.arange(t // BLOCK))
    return o.transpose(1, 0, 2, 3).reshape(bsz, t, C_HEADS * C_V)

def swiglu(h, w1, w3, w2):
    return (jax.nn.silu(h @ w1) * (h @ w3)) @ w2

def moe_ffn(h, wr, br, w1, w3, w2):
    logits = (h @ wr).astype(jnp.float32) + br.astype(jnp.float32)
    top_v, top_i = lax.top_k(logits, TOP_K)
    top_w = jax.nn.softmax(top_v, axis=-1)
    gates = jnp.sum(jax.nn.one_hot(top_i, N_EXPERTS, dtype=jnp.float32) * top_w[..., None], axis=-2).astype(h.dtype)
    y = jnp.zeros_like(h)
    for e in range(N_EXPERTS):
        y = y + gates[..., e:e + 1] * swiglu(h, w1[e], w3[e], w2[e])
    return y

def setup_inputs(seed: int = 0) -> dict:
    key = jax.random.key(seed)
    ks = iter(jax.random.split(key, 40))

    def nrm(shape, scale):
        return jax.random.normal(next(ks), shape, jnp.float32) * scale

    def gain(shape):
        return 1.0 + nrm(shape, 0.05)

    D = D_MODEL
    n_dense = (DEPTH + 1) // 2
    n_moe = DEPTH // 2
    return {
        "x": nrm((BATCH, SEQ, D), 1.0),
        "c": nrm((BATCH, D), 1.0),
        "ctx": nrm((BATCH, CTX_LEN, D), 1.0),
        "c_ctx": nrm((D,), 1.0),
        "ada_w": nrm((DEPTH, D, 6 * D), 0.5 * D ** -0.5),
        "ada_b": nrm((DEPTH, 6 * D), 0.02),
        "mix_norm_g": gain((DEPTH, D)),
        "ffn_norm_g": gain((DEPTH, D)),
        "w_in": nrm((DEPTH, D, IN_COLS), D ** -0.5),
        "w_out": nrm((DEPTH, MIX_WIDTH, D), MIX_WIDTH ** -0.5),
        "a_q_norm_g": gain((DEPTH, HEAD_DIM)),
        "a_k_norm_g": gain((DEPTH, HEAD_DIM)),
        "a_sink": nrm((DEPTH, A_HEADS), 1.0),
        "b_conv_w": nrm((DEPTH, B_WIDTH, B_CH), B_WIDTH ** -0.5),
        "b_conv_b": nrm((DEPTH, B_CH), 0.02),
        "b_ln_g": gain((DEPTH, B_CH)),
        "b_ln_b": nrm((DEPTH, B_CH), 0.02),
        "c_q_rank_norm_g": gain((DEPTH, C_Q_RANK)),
        "c_kv_rank_norm_g": gain((DEPTH, C_KV_RANK)),
        "c_w_uq": nrm((DEPTH, C_Q_RANK, C_HEADS * (C_NOPE + C_ROPE)), C_Q_RANK ** -0.5),
        "c_w_ukv": nrm((DEPTH, C_KV_RANK, C_HEADS * (C_NOPE + C_V)), C_KV_RANK ** -0.5),
        "c_q_nope_norm_g": gain((DEPTH, C_NOPE)),
        "c_k_nope_norm_g": gain((DEPTH, C_NOPE)),
        "c_q_rope_norm_g": gain((DEPTH, C_ROPE)),
        "c_k_rope_norm_g": gain((DEPTH, C_ROPE)),
        "dense_w1": nrm((n_dense, D, D_FF), D ** -0.5),
        "dense_w3": nrm((n_dense, D, D_FF), D ** -0.5),
        "dense_w2": nrm((n_dense, D_FF, D), D_FF ** -0.5),
        "moe_router_w": nrm((n_moe, D, N_EXPERTS), D ** -0.5),
        "moe_router_b": nrm((n_moe, N_EXPERTS), 0.01),
        "moe_w1": nrm((n_moe, N_EXPERTS, D, D_FF), D ** -0.5),
        "moe_w3": nrm((n_moe, N_EXPERTS, D, D_FF), D ** -0.5),
        "moe_w2": nrm((n_moe, N_EXPERTS, D_FF, D), D_FF ** -0.5),
    }

def reference(x, c, ctx, c_ctx, ada_w, ada_b, mix_norm_g, ffn_norm_g, w_in, w_out,
              a_q_norm_g, a_k_norm_g, a_sink, b_conv_w, b_conv_b, b_ln_g, b_ln_b,
              c_q_rank_norm_g, c_kv_rank_norm_g, c_w_uq, c_w_ukv,
              c_q_nope_norm_g, c_k_nope_norm_g, c_q_rope_norm_g, c_k_rope_norm_g,
              dense_w1, dense_w3, dense_w2, moe_router_w, moe_router_b, moe_w1, moe_w3, moe_w2):
    bsz, t = x.shape[:2]
    ROWS = t // GRID_W
    rows = jnp.repeat(jnp.arange(ROWS), GRID_W)
    cols = jnp.arange(ROWS * GRID_W) % GRID_W
    tab_a = axial_tables(rows, cols, HEAD_DIM, x.dtype)
    tab_c = axial_tables(rows, cols, C_ROPE, x.dtype)
    c_act = jax.nn.silu(c)
    cc_act = jax.nn.silu(c_ctx)

    for i in range(DEPTH):
        last = i == DEPTH - 1
        mod_x = (c_act @ ada_w[i] + ada_b[i]).reshape(bsz, 6, 1, D_MODEL)
        mod_c = (cc_act @ ada_w[i] + ada_b[i]).reshape(6, 1, 1, D_MODEL)

        hx = modulate(rms_norm(x, mix_norm_g[i]), mod_x[:, 0], mod_x[:, 1])
        hc = modulate(rms_norm(ctx, mix_norm_g[i]), mod_c[0], mod_c[1])
        gparams = (a_q_norm_g[i], a_k_norm_g[i], c_q_rank_norm_g[i], c_kv_rank_norm_g[i], c_w_uq[i], c_w_ukv[i],
                   c_q_nope_norm_g[i], c_k_nope_norm_g[i], c_q_rope_norm_g[i], c_k_rope_norm_g[i])
        qa_x, ka_x, va_x, ub_x, qn_x, qr_x, kn_x, kr_x, vc_x = mixer_inputs(hx @ w_in[i], *gparams)
        qa_c, ka_c, va_c, ub_c, qn_c, qr_c, kn_c, kr_c, vc_c = mixer_inputs(hc @ w_in[i], *gparams)

        qa_x = rope_2d(qa_x, tab_a)
        ka_x = rope_2d(ka_x, tab_a)
        qr_x = rope_2d(qr_x, tab_c)
        kr_x = rope_2d(kr_x[:, :, None, :], tab_c)[:, :, 0, :]

        o_a = window_attention(qa_x, ka_x, va_x, ka_c, va_c, a_sink[i])
        o_b = conv_module(ub_x, b_conv_w[i], b_conv_b[i], b_ln_g[i], b_ln_b[i])
        o_c = mla_blocks(qn_x, qr_x, jnp.concatenate([kn_x, kn_c], axis=1),
                         jnp.concatenate([kr_x, kr_c], axis=1),
                         jnp.concatenate([vc_x, vc_c], axis=1))
        x = x + mod_x[:, 2] * (jnp.concatenate([o_a, o_b, o_c], axis=-1) @ w_out[i])
        if not last:
            oc_a = ctx_gqa(qa_c, ka_c, va_c, a_sink[i])
            oc_b = conv_module(ub_c, b_conv_w[i], b_conv_b[i], b_ln_g[i], b_ln_b[i])
            oc_c = mla_core(qn_c, qr_c, kn_c, kr_c, vc_c)
            ctx = ctx + mod_c[2] * (jnp.concatenate([oc_a, oc_b, oc_c], axis=-1) @ w_out[i])

        j = i // 2
        if i % 2 == 0:
            ffn = lambda h, j=j: swiglu(h, dense_w1[j], dense_w3[j], dense_w2[j])
        else:
            ffn = lambda h, j=j: moe_ffn(h, moe_router_w[j], moe_router_b[j], moe_w1[j], moe_w3[j], moe_w2[j])
        x = x + mod_x[:, 5] * ffn(modulate(rms_norm(x, ffn_norm_g[i]), mod_x[:, 3], mod_x[:, 4]))
        if not last:
            ctx = ctx + mod_c[5] * ffn(modulate(rms_norm(ctx, ffn_norm_g[i]), mod_c[3], mod_c[4]))

    return x


_drawn_inputs = setup_inputs


def setup_inputs(seed=0):
    import zlib

    import numpy as np

    out = dict(_drawn_inputs(seed))
    spreads = {}
    factors = {'mix_norm_g': 6.302,
     'a_q_norm_g': 8.0,
     'a_k_norm_g': 8.0,
     'a_sink': 8.0,
     'b_conv_b': 6.145,
     'b_ln_g': 4.178,
     'b_ln_b': 8.0,
     'c_q_rank_norm_g': 8.0,
     'c_kv_rank_norm_g': 8.0,
     'c_w_uq': 2.783,
     'c_q_nope_norm_g': 8.0,
     'c_k_nope_norm_g': 8.0,
     'c_q_rope_norm_g': 8.0,
     'c_k_rope_norm_g': 8.0,
     'moe_router_b': 25.066}
    for name, (base, spread) in spreads.items():
        noise = np.random.default_rng([zlib.crc32(name.encode()), seed]).standard_normal(out[name].shape)
        drawn = base * np.exp(spread * noise) if base else spread * noise
        out[name] = __import__('jax').numpy.asarray(drawn.astype(out[name].dtype))
    for name, factor in factors.items():
        out[name] = (out[name] * factor).astype(out[name].dtype)
    return out
```

```python
from contextlib import ExitStack

import numpy as np
import concourse.bass as bass
from concourse import mybir

ALU = mybir.AluOpType
ACT = mybir.ActivationFunctionType
AX = mybir.AxisListType
F32 = mybir.dt.float32
I32 = mybir.dt.int32
U32 = mybir.dt.uint32

P = 128
D = 1024
KD = D // P
NX, NC_TOK = 256, 256
T = NX + NC_TOK
DEPTH = 2
GRID_W = 64
HD = 64
A_HEADS, A_KV = 8, 2
B_CH, TAPS = 256, 31
HALO = TAPS // 2
C_HEADS, C_NOPE, C_ROPE, C_V = 4, 64, 32, 64
C_QK = C_NOPE + C_ROPE
C_Q_RANK, C_KV_RANK = 384, 256
FF = 2816
FT = FF // P
NE = 8
EPS = 1e-6
NEG = -1e30
A_SCALE = HD ** -0.5
C_SCALE = C_QK ** -0.5
WINDOW = 128

UNIT = 2048
RING = 11
ADA_U = 6 * D // 256
IN_U, OUT_U = 9, 4
UP_U, DOWN_U = FT, FT * KD // 16
EXP_U = 3 * FF // 256
A_Q0, A_K0, A_V0, U_A0, U_G0, CQ0, CKV0, KR0 = 0, 512, 640, 768, 1024, 1280, 1664, 1920
TILES = (["ua0", "ua1", "ug0", "ug1", "ckv0", "ckv1", "cq0", "cq1", "cq2", "ka", "va", "qa0", "qa1", "qa2", "qa3", "kr",
          "kn0", "kn1", "vc0", "vc1", "qc0", "qc1", "qc2", "qc3"])
COL0 = {"ua0": U_A0, "ua1": U_A0 + P, "ug0": U_G0, "ug1": U_G0 + P, "ckv0": CKV0, "ckv1": CKV0 + P,
        "cq0": CQ0, "cq1": CQ0 + P, "cq2": CQ0 + 2 * P, "ka": A_K0, "va": A_V0,
        "qa0": A_Q0, "qa1": A_Q0 + P, "qa2": A_Q0 + 2 * P, "qa3": A_Q0 + 3 * P, "kr": KR0}
GROUPS = [(("ckv0", "ckv1"), "rank", False), (("cq0", "cq1", "cq2"), "rank", False), (("ka",), "head", True),
          (("qa0",), "head", True), (("qa1",), "head", True), (("qa2",), "head", True), (("qa3",), "head", True),
          (("kr",), "krope", True), (("kn0",), "head", False), (("kn1",), "head", False),
          (("qc0",), "mla", True), (("qc1",), "mla", True), (("qc2",), "mla", True), (("qc3",), "mla", True)]
GROUP_OF = {t: g for g, (ts, _, _) in enumerate(GROUPS) for t in ts}
NORMED = [t for t in TILES if t in GROUP_OF]
ROPED = [g for g, (_, _, roped) in enumerate(GROUPS) if roped]
ADA_G = ADA_U // 4
ADA_AFTER_TILE = {3: 2, 7: 3, 11: 4, 23: 5}
ADA_AFTER_UP = {1: 0, 4: 1, 7: 2, 10: 3, 13: 4, 16: 5}


def stream_plan():
    plan = [("ada", 0, u) for u in range(8)]
    for t in range(IN_U):
        plan.append(("in", 0, t))
        g = {1: 2, 3: 3, 5: 4, 8: 5}.get(t)
        if g is not None:
            plan += [("ada", 0, 4 * g + j) for j in range(4)]
    plan += [("out", 0, u) for u in range(OUT_U)]
    for f in range(UP_U):
        plan.append(("up", 0, f))
        if f in ADA_AFTER_UP:
            plan += [("ada", 1, 4 * ADA_AFTER_UP[f] + j) for j in range(4)]
    plan += [("down", 0, u) for u in range(DOWN_U)]
    plan += [("in", 1, t) for t in range(IN_U)] + [("out", 1, u) for u in range(OUT_U)]
    return plan


PLAN = stream_plan()
UNIT_AT = {u: n for n, u in enumerate(PLAN)}
FRONT = len(PLAN)
ALL_U = FRONT + NE * EXP_U



def columns(sizes):
    at, n = {}, 0
    for name, size in sizes:
        at[name] = (n, n + size)
        n += size
    return at, n


CONST_AT, CONST_W = columns([("ident", P), ("head", P), ("mla", P), ("ones", P), ("rot_a", P), ("rot_c", P),
                             ("cos_a", NX), ("sin_a", NX), ("cos_c", NX), ("sin_c", NX), ("mask0", P), ("mask1", P),
                             ("before", P), ("slots", 2 * P), ("eight", NE), ("eps", 1)])
PAR_AT, PAR_W = columns([("mix_g", KD), ("ffn_g", KD), ("ada_b", 6 * KD), ("q_g", 1), ("k_g", 1), ("cq_g", 3),
                         ("ckv_g", 2), ("qc_g", 1), ("kn_g", 1), ("kr_g", 1), ("conv_w", 2 * TAPS), ("conv_b", 2),
                         ("ln_g", 2), ("ln_b", 2), ("sink", A_HEADS)])
MOEP_AT, MOEP_W = columns([("router", KD * NE), ("router_b", NE)])

ITEMS = NE + 3
NI = ITEMS + 1
META_W = 2 * NI + 8


def numbering(keys):
    return {k: n + 1 for n, k in enumerate(keys)}


def attention_units(layer):
    out = []
    for kind, pairs in (("A", 4), ("C", 2)):
        for pair in range(pairs):
            for stream in range(2 if layer == 0 else 1):
                for q in range(2):
                    out.append((kind, pair, stream, q))
    return out


def backbone(nc, stream, consts, params, moe_params, c_cols, x_t, out_t):
    with ExitStack() as ctx:
        def sb(name, shape, dt=F32):
            return ctx.enter_context(nc.sbuf_tensor(name, shape, dt))

        def sem(name):
            return ctx.enter_context(nc.semaphore(name))

        ring = sb("ring", [P, RING, UNIT])
        xT = sb("xT", [P, KD, T])
        hT = sb("hT", [P, KD, T])
        cst = sb("cst", [P, CONST_W])
        par = sb("par", [P, DEPTH, PAR_W])
        moep = sb("moep", [P, MOEP_W])
        ccol = sb("ccol", [P, KD, 2])
        csig = sb("csig", [P, KD, 2])
        cact = sb("cact", [P, KD, 32])
        mod = sb("mod", [P, DEPTH, 2, 6 * KD])
        acol = sb("acol", [P, 4, 2, KD])
        nsink = sb("nsink", [P, DEPTH, A_HEADS])
        adarow = sb("adarow", [P, 256])
        sq = sb("sq", [P, 2, T])
        rr = sb("rr", [P, 2, T])
        lnr = sb("lnr", [P, T])
        tmp = sb("tmp", [P, 2, T])
        small = sb("small", [P, 64])
        arena = sb("arena", [P, 14976])

        def carve():
            at = [0]

            def take(*shape):
                n = int(np.prod(shape))
                v = arena[:, at[0]:at[0] + n]
                at[0] += n
                assert at[0] <= 14976, at[0]
                if len(shape) == 2:
                    v = v.rearrange("p (a b) -> p a b", b=shape[1])
                if len(shape) == 3:
                    v = v.rearrange("p (a b c) -> p a b c", b=shape[1], c=shape[2])
                return v
            return take

        take = carve()
        qA, kA = take(4, T), take(2, T)
        vA = take(4, P)
        qC, kC = take(C_HEADS, T), take(C_HEADS, T)
        vC = take(4, C_HEADS * C_V)
        upad = take(2, 2, NX + 2 * HALO)
        yconv = take(2, T)
        pool = take(8, T)
        probs, probs_t = pool[:, 0:4, :], pool[:, 4:8, :]
        kraw = pool[:, 0:2, :]
        cqn, ckvn = pool[:, 2:5, :], pool[:, 5:7, :]
        krb = pool[:, 7, :]
        take = carve()
        hid = take(FT, T)
        act_s = take(2, T)
        take = carve()
        htok = take(2, D)
        yT = take(KD, NX)
        hTe = take(KD, P)
        gTe = take(FT, P)
        outE = take(1, D)[:, 0, :]
        sel = take(2, P)
        selg = take(2, P)
        selg_t = take(1, NX)[:, 0, :]
        s_e = take(2, 256)
        g_e = take(2, 256)
        rt = take(1, 512)[:, 0, :]
        pos = take(2, NI)
        rt_at, _ = columns([("lg", 16), ("top", 16), ("idx", 16), ("hot0", 16), ("hot1", 16), ("mask", 16), ("gates", 16),
                            ("place", 16), ("pick", 16), ("gap", 2), ("gap_e", 2), ("den", 2), ("w0", 2), ("w1", 2),
                            ("two", 2), ("count", 8), ("over", 8), ("upto", 8), ("rank", 8), ("is_x", 8), ("one8", 8)])

        def rtab(name):
            lo, hi = rt_at[name]
            v = rt[:, lo:hi]
            return v.rearrange("p (t e) -> p t e", t=2) if hi - lo == 16 else v

        gate = take(2, NI)
        meta_f = take(1, META_W)[:, 0, :]
        meta = sb("meta", [P, META_W], I32)
        idx8 = sb("idx8", [P, 2, 8], U32)
        mx = sb("mx", [P, 2, 2])
        nm = sb("nm", [P, 2, 2])
        den = sb("den", [P, 2, 2])
        es = sb("es", [P, 2, 2])
        rden = sb("rden", [P, 2])
        sm = sb("sm", [P, 2, 2])
        dsum = sb("dsum", [P, 2])

        ps = ctx.enter_context(nc.psum_tensor("ps", [P, 8, 512], F32))

        def c_(name, a=None, b=None):
            lo, hi = CONST_AT[name]
            return cst[:, lo + (a or 0):hi if b is None else lo + b]

        def p_(layer, name, i=0, n=1):
            lo, _ = PAR_AT[name]
            return par[:, layer, lo + i:lo + i + n]

        slot_loaded = [sem(f"slot_loaded{i}") for i in range(RING)]
        ring_used = sem("ring_used")
        small_loaded = sem("small_loaded")
        x_loaded = sem("x_loaded")
        cact_ready = sem("cact_ready")
        ada_mm, ada_row, ada_tr, ada_mod = sem("ada_mm"), sem("ada_row"), sem("ada_tr"), sem("ada_mod")
        acol_ready = sem("acol_ready")
        sqx_ready, ssx_read, ssx_done = sem("sqx_ready"), sem("ssx_read"), sem("ssx_done")
        rx_ready, tx_ready, hx_ready = sem("rx_ready"), sem("tx_ready"), sem("hx_ready")
        mm_done, raw_done, sq_done, ss_read = sem("mm_done"), sem("raw_done"), sem("sq_done"), sem("ss_read")
        ln_done, r_ready, nrm_done, rot_done, rope_done = (sem("ln_done"), sem("r_ready"), sem("nrm_done"),
                                                          sem("rot_done"), sem("rope_done"))
        spread_done = sem("spread_done")
        pad_ready = sem("pad_ready")
        s_done, max_done, exp_done, soft_done = sem("s_done"), sem("max_done"), sem("exp_done"), sem("soft_done")
        tr_done, trc_act, trc_dve, pv_done, o_done = (sem("tr_done"), sem("trc_act"), sem("trc_dve"), sem("pv_done"),
                                                      sem("o_done"))
        conv_step, dve_step, act_step = sem("conv_step"), sem("dve_step"), sem("act_step")
        mu_done, dev_done, dsq_done, var_done, lnr_ready, z_done, sig_done, ob_done = (
            sem("mu_done"), sem("dev_done"), sem("dsq_done"), sem("var_done"), sem("lnr_ready"), sem("z_done"),
            sem("sig_done"), sem("ob_done"))
        wo_done, res_done = sem("wo_done"), sem("res_done")
        up_done, silu_done, hid_done = sem("up_done"), sem("silu_done"), sem("hid_done")
        meta_ready, final_done, out_stored = sem("meta_ready"), sem("final_done"), sem("out_stored")
        logit_mm, htok_mm, htok_act, htok_dve, mask_ready, count_mm = (
            sem("logit_mm"), sem("htok_mm"), sem("htok_act"), sem("htok_dve"), sem("mask_ready"), sem("count_mm"))
        gap_ready, gap_exp = sem("gap_ready"), sem("gap_exp")
        sel_ready, gather_mm, hte_act, hte_dve = sem("sel_ready"), sem("gather_mm"), sem("hte_act"), sem("hte_dve")
        selgt_mm, selgt_done = sem("selgt_mm"), sem("selgt_done")
        eup_mm, se_done, ge_done, gt_mm, gte_done = (sem("eup_mm"), sem("se_done"), sem("ge_done"), sem("gt_mm"),
                                                    sem("gte_done"))
        acc_mm, oute_act, oute_dve, scatter_mm, y_done = (sem("acc_mm"), sem("oute_act"), sem("oute_dve"),
                                                          sem("scatter_mm"), sem("y_done"))

        def nq(layer, tile):
            keys = tile.startswith(("k", "v", "ckv"))
            return T if layer == 0 or keys else NX

        LT = [(layer, t) for layer in range(DEPTH) for t in TILES]
        mm_at = numbering(LT)
        normed_at = numbering([(layer, t) for layer in range(DEPTH) for t in NORMED])
        group_at = numbering([(layer, g) for layer in range(DEPTH) for g in range(len(GROUPS))])
        roped_at = numbering([(layer, g) for layer in range(DEPTH) for g in ROPED])
        ada_at = numbering([(layer, g) for layer in range(DEPTH) for g in range(ADA_G)])
        ATT = [(layer, n) for layer in range(DEPTH) for n in range(len(attention_units(layer)))]
        att_at = numbering(ATT)
        STREAMS = [2, 1]
        CONV_AT = [(1, 3), (1, 3)]
        CONV_STEPS = [2 * TAPS, 4 * TAPS]
        NORM_S = [2, 2, 2, 1]
        norm_h_at = numbering([(n, k, s) for n in range(4) for k in range(KD) for s in range(NORM_S[n])])
        norm_sq_at = numbering([(n, k) for n in range(4) for k in range(KD)])
        res_at = numbering([(w, k) for w in range(3) for k in range(KD)])
        MAIN_BANK = lambda n: n % 3
        SS_BANK = lambda n: 3 + n % 2
        ROT_BANK, ADA_BANK, ADAT_BANK = 5, 6, 7

        block = ctx.enter_context(nc.Block())

        @block.sync
        def _(sp):
            def unit(n, dst):
                sp.dma_start(ring[:, dst, :], stream[n, :, :]).then_inc(slot_loaded[dst], 16)

            for s in range(RING):
                unit(s, s)
            with sp.Fori(1, ALL_U // RING) as r:
                for s in range(RING):
                    sp.wait_ge(ring_used, r * RING + (s + 1 - RING))
                    sp.dma_start(ring[:, s, :], stream[bass.ds(r * RING + s, 1), :, :].rearrange("a p n -> (a p) n")
                                 ).then_inc(slot_loaded[s], 16)
            done = ALL_U // RING * RING
            for n in range(done, ALL_U):
                sp.wait_ge(ring_used, n + 1 - RING)
                unit(n, n % RING)
            sp.wait_ge(meta_ready, 1)
            extra = sp.value_load(meta[0:1, NI + 4:NI + 5], min_val=0, max_val=3)
            with sp.If(extra > 0):
                with sp.Fori(0, extra) as x:
                    expert = sp.value_load(meta[0:1, bass.ds(x + NI, 1)], min_val=0, max_val=NE - 1)
                    for u in range(EXP_U):
                        s = (ALL_U + u) % RING
                        sp.wait_ge(ring_used, x * EXP_U + (ALL_U + u + 1 - RING))
                        sp.dma_start(ring[:, s, :], stream[bass.ds(expert * EXP_U + (FRONT + u), 1), :, :]
                                     .rearrange("a p n -> (a p) n")).then_inc(slot_loaded[s], 16)
            sp.wait_ge(final_done, 1)
            sp.dma_start(out_t, yT).then_inc(out_stored, 16)
            sp.wait_ge(out_stored, 16)

        @block.tensor
        def _(pe):
            owed = [0]

            def first(ins):
                if owed[0]:
                    ins.then_inc(ring_used, owed[0])
                    owed[0] = 0

            def arrived(key):
                n = UNIT_AT[key]
                pe.wait_ge(slot_loaded[n % RING], 16 * (n // RING + 1))
                return n % RING

            def ada_rows(layer, g):
                n = ada_at[layer, g]
                slots = [arrived(("ada", layer, 4 * g + j)) for j in range(4)]
                if n > 1:
                    pe.wait_ge(ada_row, n - 1)
                for k in range(KD):
                    for j in range(4):
                        last = pe.matmul(ps[32 * j:32 * j + 32, ADA_BANK, 0:256], cact[:, k, :],
                                         ring[:, slots[j], k * 256:(k + 1) * 256], start=(k == 0), stop=(k == KD - 1))
                        first(last)
                last.then_inc(ada_mm, 1)
                owed[0] += 4

            def ada_turn(layer, g):
                n = ada_at[layer, g]
                pe.wait_ge(ada_row, n)
                if n > 1:
                    pe.wait_ge(ada_mod, n - 1)
                for half in range(2):
                    last = pe.transpose(ps[:, ADAT_BANK, half * P:(half + 1) * P],
                                        adarow[:, half * P:(half + 1) * P], c_("ident"))
                last.then_inc(ada_tr, 1)

            def sum_squares(norm, k):
                n = norm_sq_at[norm, k]
                pe.wait_ge(sqx_ready, n)
                w = NX if norm == 3 else T
                pe.matmul(ps[:, SS_BANK(0), 0:w], c_("ones"), sq[:, k % 2, 0:w], start=(k == 0), stop=(k == KD - 1)
                          ).then_inc(ssx_read, 1)

            def project(layer, t):
                tile = TILES[t]
                n = mm_at[layer, tile]
                bank = MAIN_BANK(n)
                w = nq(layer, tile)
                if n > 3:
                    pe.wait_ge(raw_done, n - 3)
                    before = LT[n - 4]
                    if before[1] in GROUP_OF:
                        pe.wait_ge(sq_done, normed_at[before])
                if t <= 15:
                    slot = arrived(("in", layer, t // 2))
                    base = t % 2 * 1024 if t != 15 else 1024
                    wide = 32 if tile == "kr" else P
                    for k in range(KD):
                        if t == 0:
                            pe.wait_ge(hx_ready, norm_h_at[2 * layer, k, 1])
                        lhs = ring[:, slot, base + k * wide:base + (k + 1) * wide]
                        if tile == "va":
                            continue
                        out = ps[64:96, bank, 0:w] if tile == "kr" else ps[:, bank, 0:w]
                        last = pe.matmul(out, lhs, hT[:, k, 0:w], start=(k == 0), stop=(k == KD - 1))
                        first(last)
                    if tile == "va":
                        for q in range(4):
                            for k in range(KD):
                                last = pe.matmul(ps[:, bank, q * P:(q + 1) * P], hT[:, k, q * P:(q + 1) * P],
                                                 ring[:, slot, base + k * P:base + (k + 1) * P],
                                                 start=(k == 0), stop=(k == KD - 1))
                                first(last)
                    last.then_inc(mm_done, 1)
                    if t % 2 and t != 15:
                        owed[0] += 1
                    return
                s7, s8 = arrived(("in", layer, 7)), arrived(("in", layer, 8))
                if tile in ("kn0", "kn1"):
                    j = int(tile[2])
                    pe.wait_ge(nrm_done, group_at[layer, 0])
                    for k in range(2):
                        wk = ring[:, s8, 384 + k * 512 + j * P:384 + k * 512 + (j + 1) * P]
                        last = pe.matmul(ps[:, bank, 0:w], wk, ckvn[:, k, 0:w],
                                         start=(k == 0), stop=(k == 1))
                elif tile in ("vc0", "vc1"):
                    j = int(tile[2])
                    for q in range(2):
                        for k in range(2):
                            wk = ring[:, s8, 384 + k * 512 + 256:384 + (k + 1) * 512]
                            tok = (2 * j + q) * P
                            last = pe.matmul(ps[:, bank, q * 256:(q + 1) * 256], ckvn[:, k, tok:tok + P],
                                             wk, start=(k == 0), stop=(k == 1))
                else:
                    h = int(tile[2])
                    pe.wait_ge(nrm_done, group_at[layer, 1])
                    for k in range(3):
                        wk = ring[:, s7, 1280 + k * 384:1280 + (k + 1) * 384] if k < 2 else ring[:, s8, 0:384]
                        last = pe.matmul(ps[0:C_QK, bank, 0:w], wk[:, h * C_QK:(h + 1) * C_QK], cqn[:, k, 0:w],
                                         start=(k == 0), stop=(k == 2))
                last.then_inc(mm_done, 1)
                if t == len(TILES) - 1:
                    owed[0] += 2

            def group_sum(layer, t):
                tile = TILES[t]
                if tile not in GROUP_OF:
                    return
                g = GROUP_OF[tile]
                tiles, kind, _ = GROUPS[g]
                gn, n = group_at[layer, g], normed_at[layer, tile]
                w = nq(layer, tile)
                pe.wait_ge(sq_done, n)
                if tile == tiles[0] and gn > 2:
                    pe.wait_ge(nrm_done, gn - 2)
                s = sq[:, n % 2, 0:w]
                kw = dict(start=(tile == tiles[0]), stop=(tile == tiles[-1]))
                if kind == "krope":
                    pe.matmul(ps[64:96, SS_BANK(gn), 0:w], c_("mla", 64, 96)[64:96, :], s[64:96, :], **kw
                              ).then_inc(ss_read, 1)
                elif kind == "mla":
                    pe.matmul(ps[0:C_QK, SS_BANK(gn), 0:w], c_("mla", 0, C_QK)[0:C_QK, :], s[0:C_QK, :], **kw
                              ).then_inc(ss_read, 1)
                else:
                    pe.matmul(ps[:, SS_BANK(gn), 0:w], c_("head" if kind == "head" else "ones"), s, **kw
                              ).then_inc(ss_read, 1)

            def rotate(layer, t):
                tile = TILES[t]
                g = GROUP_OF.get(tile)
                if g is None or not GROUPS[g][2]:
                    return
                n = roped_at[layer, g]
                pe.wait_ge(nrm_done, group_at[layer, g])
                if n > 1:
                    pe.wait_ge(rope_done, n - 1)
                if tile == "kr":
                    pe.matmul(ps[64:96, ROT_BANK, 0:NX], c_("rot_c", 64, 96)[64:96, :], krb[64:96, 0:NX],
                              start=True, stop=True).then_inc(rot_done, 1)
                elif tile.startswith("qc"):
                    pe.matmul(ps[0:C_QK, ROT_BANK, 0:NX], c_("rot_c", 0, C_QK)[0:C_QK, :], qC[0:C_QK, int(tile[2]), 0:NX],
                              start=True, stop=True).then_inc(rot_done, 1)
                else:
                    src = kraw[:, 0, 0:NX] if tile == "ka" else qA[:, int(tile[2]), 0:NX]
                    pe.matmul(ps[:, ROT_BANK, 0:NX], c_("rot_a"), src, start=True, stop=True).then_inc(rot_done, 1)

            def projections(layer):
                for t in range(len(TILES)):
                    project(layer, t)
                    if t >= 1:
                        group_sum(layer, t - 1)
                    if t >= 2:
                        rotate(layer, t - 2)
                    if layer == 0 and t in ADA_AFTER_TILE:
                        ada_rows(0, ADA_AFTER_TILE[t])
                    if layer == 0 and t - 1 in ADA_AFTER_TILE:
                        ada_turn(0, ADA_AFTER_TILE[t - 1])
                group_sum(layer, len(TILES) - 1)
                rotate(layer, len(TILES) - 2)
                if layer == 0:
                    ada_turn(0, ADA_G - 1)
                rotate(layer, len(TILES) - 1)

            def scores(layer, a):
                kind, pair, stream_, q = attention_units(layer)[a]
                n = att_at[layer, a]
                lo = stream_ * NX
                q0 = lo + q * P
                if n > 2:
                    pe.wait_ge(exp_done, n - 2)
                for hh in range(2):
                    out = ps[:, 2 * (n % 2) + hh, 0:T - lo]
                    if kind == "A":
                        r = slice(64 * hh, 64 * hh + 64)
                        last = pe.matmul(out, qA[r, pair, q0:q0 + P], kA[r, pair // 2, lo:T], start=True, stop=True)
                    else:
                        h = 2 * pair + hh
                        last = pe.matmul(out, qC[0:C_QK, h, q0:q0 + P], kC[0:C_QK, h, lo:T], start=True, stop=True)
                    if hh == 0:
                        first(last)
                last.then_inc(s_done, 1)

            def turn_probs(layer, a):
                _, _, stream_, _ = attention_units(layer)[a]
                n = att_at[layer, a]
                pe.wait_ge(soft_done, n)
                if n > 1:
                    pe.wait_ge(trc_act, n - 1)
                    pe.wait_ge(trc_dve, n - 1)
                for hh in range(2):
                    for b in range(4 - 2 * stream_):
                        last = pe.transpose(ps[:, 4 + hh, b * P:(b + 1) * P], probs[:, 2 * (n % 2) + hh, b * P:(b + 1) * P], c_("ident"))
                last.then_inc(tr_done, 1)

            def values(layer, a):
                kind, pair, stream_, _ = attention_units(layer)[a]
                n = att_at[layer, a]
                pe.wait_ge(trc_act, n)
                pe.wait_ge(trc_dve, n)
                if n > 1:
                    pe.wait_ge(o_done, n - 1)
                nb = 4 - 2 * stream_
                for b in range(nb):
                    for hh in range(2):
                        kt = b + 2 * stream_
                        if kind == "A":
                            v = vA[:, kt, 64 * (pair // 2):64 * (pair // 2) + 64]
                        else:
                            v = vC[:, kt, 64 * (2 * pair + hh):64 * (2 * pair + hh) + 64]
                        last = pe.matmul(ps[64 * hh:64 * hh + 64, 6, 0:P], v, probs_t[:, 2 * (n % 2) + hh, b * P:(b + 1) * P],
                                         start=(b == 0), stop=(b == nb - 1))
                last.then_inc(pv_done, 1)

            def attention(layer):
                units = attention_units(layer)
                pe.wait_ge(raw_done, mm_at[layer, TILES[-1]])
                pe.wait_ge(rope_done, roped_at[layer, ROPED[-1]])
                pe.wait_ge(spread_done, 2 * (layer + 1))
                if layer == 0:
                    pe.wait_ge(ada_mod, ada_at[0, ADA_G - 1])
                scores(layer, 0)
                scores(layer, 1)
                mean_at, var_at = CONV_AT[layer]
                for a in range(len(units)):
                    turn_probs(layer, a)
                    if a + 2 < len(units):
                        scores(layer, a + 2)
                    values(layer, a)
                    w = NX * STREAMS[layer]
                    if a == mean_at:
                        pe.wait_ge(conv_step, CONV_STEPS[layer])
                        for c in range(2):
                            last = pe.matmul(ps[:, 7, 0:w], c_("ones"), yconv[:, c, 0:w], start=(c == 0), stop=(c == 1))
                        last.then_inc(mu_done, 1)
                    if a == var_at:
                        for c in range(2):
                            pe.wait_ge(dsq_done, 2 * layer + c + 1)
                            last = pe.matmul(ps[:, 7, 0:w], c_("ones"), sq[:, c, 0:w], start=(c == 0), stop=(c == 1))
                        last.then_inc(var_done, 1)

            def mixer_out(layer):
                w = NX * STREAMS[layer]
                pe.wait_ge(o_done, att_at[layer, len(attention_units(layer)) - 1])
                pe.wait_ge(ob_done, 2 * layer + 2)
                pe.wait_ge(exp_done, att_at[layer, len(attention_units(layer)) - 1])
                for d in range(KD):
                    slot = arrived(("out", layer, d // 2))
                    n = res_at[2 * layer, d]
                    if d >= 2:
                        pe.wait_ge(res_done, n - 2)
                    for k in range(KD):
                        last = pe.matmul(ps[:, d % 2, 0:w], ring[:, slot, d % 2 * 1024 + k * P:d % 2 * 1024 + (k + 1) * P],
                                         hT[:, k, 0:w], start=(k == 0), stop=(k == KD - 1))
                        first(last)
                    last.then_inc(wo_done, 1)
                    if d % 2:
                        owed[0] += 1
                    if d >= 1:
                        sum_squares(2 * layer + 1, d - 1)
                sum_squares(2 * layer + 1, KD - 1)

            def dense():
                for f in range(FT):
                    slot = arrived(("up", 0, f))
                    if f >= 2:
                        pe.wait_ge(hid_done, f - 1)
                    for m in range(2):
                        for k in range(KD):
                            if f == 0 and m == 0:
                                pe.wait_ge(hx_ready, norm_h_at[1, k, 1])
                            last = pe.matmul(ps[:, 2 * m + f % 2, :],
                                             ring[:, slot, m * 1024 + k * P:m * 1024 + (k + 1) * P], hT[:, k, :],
                                             start=(k == 0), stop=(k == KD - 1))
                            first(last)
                    last.then_inc(up_done, 1)
                    owed[0] += 1
                    if f in ADA_AFTER_UP:
                        ada_rows(1, ADA_AFTER_UP[f])
                    if f - 1 in ADA_AFTER_UP:
                        ada_turn(1, ADA_AFTER_UP[f - 1])
                for d in range(KD):
                    n = res_at[1, d]
                    if d >= 2:
                        pe.wait_ge(res_done, n - 2)
                    for f in range(FT):
                        b = d * FT + f
                        if b % 16 == 0:
                            slot = arrived(("down", 0, b // 16))
                        if d == 0:
                            pe.wait_ge(hid_done, f + 1)
                        last = pe.matmul(ps[:, 4 + d % 2, :], ring[:, slot, b % 16 * P:(b % 16 + 1) * P], hid[:, f, :],
                                         start=(f == 0), stop=(f == FT - 1))
                        if f != FT - 1:
                            first(last)
                        if b % 16 == 15:
                            owed[0] += 1
                    last.then_inc(wo_done, 1)
                    if d >= 1:
                        sum_squares(2, d - 1)
                sum_squares(2, KD - 1)

            pe.wait_ge(small_loaded, 16 * 5)
            for k in range(KD):
                sum_squares(0, k)
            pe.wait_ge(cact_ready, 1)
            for g in range(2):
                ada_rows(0, g)
                ada_turn(0, g)
            projections(0)
            attention(0)
            mixer_out(0)
            dense()
            projections(1)
            attention(1)
            mixer_out(1)
            def unit_wait(u, i):
                n = FRONT + u
                pe.wait_ge(slot_loaded[n % RING], i * (16 * EXP_U // RING) + 16 * (n // RING + 1))
                return n % RING

            def gather():
                for d in range(KD):
                    for tt in range(2):
                        last = pe.matmul(ps[:, 6 + d // 4, d % 4 * P:(d % 4 + 1) * P], htok[:, tt, d * P:(d + 1) * P],
                                         sel[:, tt, :], start=(tt == 0), stop=(tt == 1))
                        first(last)
                last.then_inc(gather_mm, 1)

            U = EXP_U // 3

            def expert(i, narrow):
                for u in range(U + 1):
                    if u < U:
                        b = u % 2
                        if u < 2:
                            pe.wait_ge(y_done, i * 4 + (u + 1))
                        else:
                            pe.wait_ge(ge_done, i * U + (u - 1))
                        if narrow:
                            s1, s3 = unit_wait(2 * u, i), unit_wait(2 * u + 1, i)
                            for k in range(KD):
                                a = pe.matmul(ps[0:64, b, 0:256], hTe[:, k, 0:64], ring[:, s1, k * 256:(k + 1) * 256],
                                              start=(k == 0), stop=(k == KD - 1))
                                first(a)
                                last = pe.matmul(ps[64:P, b, 0:256], hTe[:, k, 0:64], ring[:, s3, k * 256:(k + 1) * 256],
                                                 start=(k == 0), stop=(k == KD - 1))
                        else:
                            for j in range(2):
                                s = unit_wait(2 * u + j, i)
                                for k in range(KD):
                                    last = pe.matmul(ps[:, b, j * 256:(j + 1) * 256], hTe[:, k, :],
                                                     ring[:, s, k * 256:(k + 1) * 256], start=(k == 0), stop=(k == KD - 1))
                                    first(last)
                        last.then_inc(eup_mm, 1)
                        owed[0] += 2
                    if u == 0:
                        pe.wait_ge(y_done, i * 4 + 4)
                        for tt in range(2):
                            last = pe.transpose(ps[:, 3, tt * P:(tt + 1) * P], selg[:, tt, :], c_("ident"))
                        last.then_inc(selgt_mm, 1)
                    else:
                        v = u - 1
                        pe.wait_ge(ge_done, i * U + (v + 1))
                        if v == 0:
                            pe.wait_ge(y_done, i * 4 + 3)
                        elif v == 1:
                            pe.wait_ge(selgt_done, i + 1)
                        else:
                            pe.wait_ge(gte_done, i * U + (v - 1))
                        for half in range(2):
                            last = pe.transpose(ps[:, 2 + v % 2, half * P:(half + 1) * P],
                                                g_e[:, v % 2, half * P:(half + 1) * P], c_("ident"))
                        last.then_inc(gt_mm, 1)
                for u in range(U):
                    s = unit_wait(2 * U + u, i)
                    pe.wait_ge(gte_done, i * U + (u + 1))
                    for n in range(2):
                        for j in range(2):
                            w2 = ring[:, s, j * 1024 + n * 512:j * 1024 + (n + 1) * 512]
                            if narrow:
                                last = pe.matmul(ps[64 * j:64 * j + 64, 4 + n, :], gTe[:, 2 * u + j, 0:64], w2,
                                                 start=(u == 0), stop=(u == U - 1))
                            else:
                                last = pe.matmul(ps[:, 4 + n, :], gTe[:, 2 * u + j, :], w2,
                                                 start=(u == 0 and j == 0), stop=(u == U - 1 and j == 1))
                            if n == 0 and j == 0:
                                first(last)
                    owed[0] += 1
                last.then_inc(acc_mm, 1)

            for tt in range(2):
                for k in range(KD):
                    if tt == 0:
                        pe.wait_ge(hx_ready, norm_h_at[3, k, 0])
                    last = pe.matmul(ps[:, 0, tt * NE:(tt + 1) * NE], hT[:, k, tt * P:(tt + 1) * P],
                                     moep[:, k * NE:(k + 1) * NE], start=(k == 0), stop=(k == KD - 1))
                    first(last)
            last.then_inc(logit_mm, 1)
            for tt in range(2):
                for k in range(KD):
                    last = pe.transpose(ps[:, 1 + 2 * tt + k // 4, k % 4 * P:(k % 4 + 1) * P], hT[:, k, tt * P:(tt + 1) * P],
                                        c_("ident"))
                    if k % 4 == 3:
                        last.then_inc(htok_mm, 1)
            pe.wait_ge(mask_ready, 1)
            for col, parts in ((0, [("before", 0)]), (NE, [("ones", 0), ("before", 1)]), (2 * NE, [("ones", 0), ("ones", 1)])):
                for j, (what, tt) in enumerate(parts):
                    last = pe.matmul(ps[:, 5, col:col + NE], c_(what), rtab("mask")[:, tt, :], start=(j == 0),
                                     stop=(j == len(parts) - 1))
            last.then_inc(count_mm, 1)
            pe.wait_ge(htok_act, 2)
            pe.wait_ge(htok_dve, 2)
            pe.wait_ge(sel_ready, 1)
            gather()
            n_items = pe.value_load(meta[0:1, NI + 3:NI + 4], min_val=NE, max_val=ITEMS)
            with pe.Fori(0, n_items) as i:
                narrow = pe.value_load(meta[0:1, bass.ds(i, 1)], min_val=0, max_val=1)
                pe.wait_ge(hte_act, i + 1)
                pe.wait_ge(hte_dve, i + 1)
                with pe.If(narrow > 0):
                    expert(i, True)
                owed[0] = 0
                with pe.Else():
                    expert(i, False)
                pe.wait_ge(sel_ready, i + 2)
                gather()
                pe.wait_ge(oute_act, i + 1)
                pe.wait_ge(oute_dve, i + 1)
                for d in range(KD):
                    last = pe.matmul(ps[:, d // 2, d % 2 * NX:(d % 2 + 1) * NX], outE[:, d * P:(d + 1) * P], selg_t[:, :],
                                     start=True, stop=True)
                    if d % 2:
                        last.then_inc(scatter_mm, 1)

        @block.scalar
        def _(act):
            steps = [0]

            def chained(ins):
                steps[0] += 1
                ins.then_inc(act_step, 1)
                act.wait_ge(act_step, steps[0])

            def squares(norm, k):
                n = norm_sq_at[norm, k]
                if norm == 0:
                    act.wait_ge(x_loaded, 16 * KD)
                else:
                    act.wait_ge(res_done, res_at[norm - 1, k])
                if n > 2:
                    act.wait_ge(ssx_read, n - 2)
                w = NX if norm == 3 else T
                act.activation(sq[:, k % 2, 0:w], xT[:, k, 0:w], ACT.Square).then_inc(sqx_ready, 1)

            def norm_root(norm):
                w = NX if norm == 3 else T
                act.wait_ge(ssx_read, norm_sq_at[norm, KD - 1])
                chained(act.activation(lnr[:, 0:w], ps[:, SS_BANK(0), 0:w], ACT.Ln, bias=c_("eps"), scale=1.0 / D))
                act.activation(rr[:, 0, 0:w], lnr[:, 0:w], ACT.Exp, scale=-0.5).then_inc(rx_ready, 1)

            def shift_in(norm):
                layer, chunk = norm // 2, 3 * (norm % 2)
                for k in range(KD):
                    for s in range(NORM_S[norm]):
                        n = norm_h_at[norm, k, s]
                        act.wait_ge(tx_ready, n)
                        act.activation(hT[:, k, s * NX:(s + 1) * NX], tmp[:, k % 2, s * NX:(s + 1) * NX], ACT.Identity,
                                       bias=mod[:, layer, s, chunk * KD + k:chunk * KD + k + 1]).then_inc(hx_ready, 1)

            def ada_copy(layer, g):
                n = ada_at[layer, g]
                act.wait_ge(ada_mm, n)
                if n > 1:
                    act.wait_ge(ada_tr, n - 1)
                act.activation(adarow[:, :], ps[:, ADA_BANK, 0:256], ACT.Copy).then_inc(ada_row, 1)

            def tile_squares(layer, t):
                tile = TILES[t]
                w = nq(layer, tile)
                if tile.startswith("ug"):
                    act.wait_ge(mm_done, mm_at[layer, tile])
                    act.activation(tmp[:, int(tile[2]), 0:w], ps[:, MAIN_BANK(mm_at[layer, tile]), 0:w], ACT.Sigmoid
                                   ).then_inc(sig_done, 1)
                    return
                if tile not in GROUP_OF:
                    return
                n = normed_at[layer, tile]
                act.wait_ge(raw_done, mm_at[layer, tile])
                if n > 2:
                    act.wait_ge(ss_read, n - 2)
                rows = {"kr": slice(64, 96)}.get(tile, slice(0, C_QK) if tile.startswith("qc") else slice(0, P))
                act.activation(sq[rows, n % 2, 0:w], ps[rows, MAIN_BANK(mm_at[layer, tile]), 0:w], ACT.Square
                               ).then_inc(sq_done, 1)

            def group_root(layer, t):
                tile = TILES[t]
                g = GROUP_OF.get(tile)
                if g is None or GROUPS[g][0][-1] != tile:
                    return
                gn = group_at[layer, g]
                kind = GROUPS[g][1]
                w = nq(layer, tile)
                rows = {"krope": slice(64, 96), "mla": slice(0, C_QK)}.get(kind, slice(0, P))
                scale = {0: 1.0 / C_KV_RANK, 1: 1.0 / C_Q_RANK}.get(g, 1.0)
                act.wait_ge(ss_read, normed_at[layer, tile])
                if gn > 2:
                    act.wait_ge(nrm_done, gn - 2)
                if gn > 1:
                    act.wait_ge(r_ready, gn - 1)
                act.activation(lnr[rows, 0:w], ps[rows, SS_BANK(gn), 0:w], ACT.Ln, bias=c_("eps")[rows, :], scale=scale
                               ).then_inc(ln_done, 1)
                act.wait_ge(ln_done, gn)
                act.activation(rr[rows, gn % 2, 0:w], lnr[rows, 0:w], ACT.Exp, scale=-0.5).then_inc(r_ready, 1)

            def projections(layer):
                for t in range(len(TILES)):
                    tile_squares(layer, t)
                    if t >= 1:
                        group_root(layer, t - 1)
                    if layer == 0 and t - 1 in ADA_AFTER_TILE:
                        ada_copy(0, ADA_AFTER_TILE[t - 1])
                group_root(layer, len(TILES) - 1)
                if layer == 0:
                    ada_copy(0, ADA_G - 1)

            def softmax(layer, a):
                kind, pair, stream_, _ = attention_units(layer)[a]
                n = att_at[layer, a]
                scale = A_SCALE if kind == "A" else C_SCALE
                w = T - stream_ * NX
                act.wait_ge(max_done, n)
                if n > 2:
                    act.wait_ge(tr_done, n - 2)
                for hh in range(2):
                    last = act.activation(probs[:, 2 * (n % 2) + hh, 0:w], ps[:, 2 * (n % 2) + hh, 0:w], ACT.Exp,
                                          bias=nm[:, n % 2, hh:hh + 1], scale=scale, accum_out=den[:, n % 2, hh:hh + 1])
                    if hh == 1 and kind == "C":
                        last.then_inc(exp_done, 1)
                if kind == "A":
                    act.activation(es[:, n % 2, :], sm[:, n % 2, :], ACT.Exp).then_inc(exp_done, 1)

            def turned(layer, a):
                n = att_at[layer, a]
                stream_ = attention_units(layer)[a][2]
                w = T - stream_ * NX
                act.wait_ge(tr_done, n)
                if n > 2:
                    act.wait_ge(pv_done, n - 2)
                act.activation(probs_t[:, 2 * (n % 2), 0:w], ps[:, 4, 0:w], ACT.Copy).then_inc(trc_act, 1)

            def conv_norm(layer):
                w = NX * STREAMS[layer]
                act.wait_ge(var_done, layer + 1)
                chained(act.activation(lnr[:, 0:w], ps[:, 7, 0:w], ACT.Ln, bias=c_("eps"), scale=1.0 / B_CH))
                act.activation(rr[:, 1, 0:w], lnr[:, 0:w], ACT.Exp, scale=-0.5).then_inc(lnr_ready, 1)

            def attention(layer):
                units = attention_units(layer)
                mean_at, var_at = CONV_AT[layer]
                w = NX * STREAMS[layer]
                softmax(layer, 0)
                for a in range(len(units)):
                    if a == var_at:
                        for c in range(2):
                            act.wait_ge(dev_done, 2 * layer + c + 1)
                            act.activation(sq[:, c, 0:w], yconv[:, c, 0:w], ACT.Square).then_inc(dsq_done, 1)
                    turned(layer, a)
                    if a == var_at + 1:
                        conv_norm(layer)
                    if a + 1 < len(units):
                        softmax(layer, a + 1)
                for c in range(2):
                    act.wait_ge(z_done, 2 * layer + c + 1)
                    act.activation(tmp[:, c, 0:w], yconv[:, c, 0:w], ACT.Sigmoid).then_inc(sig_done, 1)

            def dense():
                for f in range(FT):
                    act.wait_ge(up_done, f + 1)
                    if f >= 2:
                        act.wait_ge(hid_done, f - 1)
                    act.activation(act_s[:, f % 2, :], ps[:, f % 2, :], ACT.Silu).then_inc(silu_done, 1)
                    if f - 1 in ADA_AFTER_UP:
                        ada_copy(1, ADA_AFTER_UP[f - 1])

            for i, (dst, src) in enumerate(((cst[:, :], consts), (par[:, 0, :], params[0]), (par[:, 1, :], params[1]),
                                            (moep[:, :], moe_params), (ccol[:, :, :], c_cols))):
                act.dma_start(dst, src).then_inc(small_loaded, 16)
            for k in range(KD):
                act.dma_start(xT[:, k, :], x_t[:, k, :]).then_inc(x_loaded, 16)
            act.wait_ge(small_loaded, 16 * 5)
            chained(act.activation(csig[:, :, :], ccol[:, :, :], ACT.Sigmoid))
            for k in range(KD):
                squares(0, k)
            norm_root(0)
            for g in range(2):
                ada_copy(0, g)
            shift_in(0)
            for layer in range(DEPTH):
                if layer:
                    for k in range(KD):
                        squares(2, k)
                    norm_root(2)
                    shift_in(2)
                projections(layer)
                attention(layer)
                for k in range(KD):
                    squares(2 * layer + 1, k)
                norm_root(2 * layer + 1)
                shift_in(2 * layer + 1)
                if layer == 0:
                    dense()
            U = EXP_U // 3

            def expert(i, narrow):
                m = 64 if narrow else P
                for u in range(U + 1):
                    if u < U:
                        act.wait_ge(eup_mm, i * U + (u + 1))
                        if u >= 2:
                            act.wait_ge(ge_done, i * U + (u - 1))
                        dst = s_e[64:P, u % 2, :] if narrow else s_e[:, u % 2, :]
                        act.activation(dst, ps[0:m, u % 2, 0:256], ACT.Silu).then_inc(se_done, 1)
                    if u >= 1:
                        v = u - 1
                        act.wait_ge(gt_mm, i * U + (v + 1))
                        act.activation(gTe[:, 2 * v:2 * v + 2, 0:m],
                                       ps[:, 2 + v % 2, 0:2 * P].rearrange("p (a b) -> p a b", a=2)[:, :, 0:m], ACT.Copy
                                       ).then_inc(gte_done, 1)

            for b in range(2):
                act.wait_ge(htok_mm, 3 + b)
                act.activation(htok[:, 1, b * 512:(b + 1) * 512], ps[:, 3 + b, :], ACT.Copy).then_inc(htok_act, 1)
            act.wait_ge(gap_ready, 1)
            act.activation(rtab("gap_e"), rtab("gap"), ACT.Exp).then_inc(gap_exp, 1)
            act.wait_ge(gather_mm, 1)
            act.activation(hTe[:, 0:4, :], ps[:, 6, :].rearrange("p (a b) -> p a b", a=4), ACT.Copy).then_inc(hte_act, 1)
            act.wait_ge(meta_ready, 1)
            n_items = act.value_load(meta[0:1, NI + 3:NI + 4], min_val=NE, max_val=ITEMS)
            with act.Fori(0, n_items) as i:
                narrow = act.value_load(meta[0:1, bass.ds(i, 1)], min_val=0, max_val=1)
                with act.If(narrow > 0):
                    expert(i, True)
                with act.Else():
                    expert(i, False)
                act.wait_ge(acc_mm, i + 1)
                act.activation(outE[:, 0:512], ps[:, 4, :], ACT.Copy).then_inc(oute_act, 1)
                act.wait_ge(gather_mm, i + 2)
                act.activation(hTe[:, 0:4, :], ps[:, 6, :].rearrange("p (a b) -> p a b", a=4), ACT.Copy
                               ).then_inc(hte_act, 1)

        @block.vector
        def _(dve):
            steps, conv, roped = [0], [0], [0]

            def chained(ins):
                steps[0] += 1
                ins.then_inc(dve_step, 1)
                dve.wait_ge(dve_step, steps[0])

            def refine(rows, buf, w, bank, count):
                t, root = tmp[rows, 0, 0:w], rr[rows, buf, 0:w]
                chained(dve.tensor_tensor(t, root, root, ALU.mult))
                chained(dve.scalar_tensor_tensor(out=t, in0=ps[rows, bank, 0:w], scalar=count * EPS, in1=t, op0=ALU.add,
                                                 op1=ALU.mult))
                chained(dve.tensor_scalar(t, t, -0.5 / count, 1.5, ALU.mult, ALU.add))
                chained(dve.tensor_tensor(root, root, t, ALU.mult))

            def ada_store(layer, g):
                n = ada_at[layer, g]
                dve.wait_ge(ada_tr, n)
                rows = ps[:, ADAT_BANK, 0:256].rearrange("p (h j s) -> p h j s", h=2, j=4)
                b = p_(layer, "ada_b", KD * g, KD).rearrange("p (j h) -> p h j", h=2)
                for s in range(2):
                    last = dve.tensor_tensor(mod[:, layer, s, KD * g:KD * (g + 1)].rearrange("p (j h) -> p h j", h=2),
                                             rows[:, :, :, s], b, ALU.add)
                last.then_inc(ada_mod, 1)
                if g in (1, 4):
                    norm = 2 * layer + g // 4
                    dve.wait_ge(ada_mod, n)
                    gain = p_(layer, "mix_g" if g == 1 else "ffn_g", 0, KD)
                    for s in range(2):
                        last = dve.scalar_tensor_tensor(out=acol[:, norm, s, :], in0=mod[:, layer, s, KD * g:KD * (g + 1)],
                                                        scalar=1.0, in1=gain, op0=ALU.add, op1=ALU.mult)
                    last.then_inc(acol_ready, 1)

            def scale_in(norm):
                dve.wait_ge(rx_ready, norm + 1)
                refine(slice(0, P), 0, NX if norm == 3 else T, SS_BANK(0), D)
                dve.wait_ge(acol_ready, norm + 1)
                for k in range(KD):
                    for s in range(NORM_S[norm]):
                        if k >= 2:
                            dve.wait_ge(hx_ready, norm_h_at[norm, k - 2, s])
                        c = slice(s * NX, (s + 1) * NX)
                        dve.scalar_tensor_tensor(out=tmp[:, k % 2, c], in0=xT[:, k, c], scalar=acol[:, norm, s, k:k + 1],
                                                 in1=rr[:, 0, c], op0=ALU.mult, op1=ALU.mult).then_inc(tx_ready, 1)

            def keep(layer, t):
                tile = TILES[t]
                n = mm_at[layer, tile]
                w = nq(layer, tile)
                bank = ps[:, MAIN_BANK(n), :]
                j = int(tile[-1]) if tile[-1].isdigit() else 0
                if tile.startswith("ug"):
                    dve.wait_ge(sig_done, 4 * layer + j + 1)
                    dve.wait_ge(raw_done, mm_at[layer, "ua1"])
                    for s in range(STREAMS[layer]):
                        c = slice(s * NX, (s + 1) * NX)
                        last = dve.tensor_tensor(upad[:, j, s, HALO:HALO + NX], yconv[:, j, c], tmp[:, j, c], ALU.mult)
                    last.then_inc(raw_done, 1)
                    return
                dve.wait_ge(mm_done, n)
                if tile.startswith("ua"):
                    ins = dve.tensor_copy(yconv[:, j, 0:w], bank[:, 0:w])
                elif tile == "va":
                    ins = dve.tensor_copy(vA, bank.rearrange("p (q c) -> p q c", q=4))
                elif tile.startswith("vc"):
                    ins = dve.tensor_copy(vC[:, 2 * j:2 * j + 2, :], bank.rearrange("p (q c) -> p q c", q=2))
                else:
                    rows, dst, gain = kept(layer, tile, j, w)
                    ins = dve.tensor_scalar(dst, bank[rows, 0:w], gain, None, ALU.mult)
                ins.then_inc(raw_done, 1)

            def kept(layer, tile, j, w):
                kind = tile.rstrip("0123")
                if kind == "ckv":
                    return slice(0, P), ckvn[:, j, 0:w], p_(layer, "ckv_g", j)
                if kind == "cq":
                    return slice(0, P), cqn[:, j, 0:w], p_(layer, "cq_g", j)
                if kind == "ka":
                    return slice(0, P), kraw[:, 0, 0:w], p_(layer, "k_g")
                if kind == "qa":
                    return slice(0, P), qA[:, j, 0:w], p_(layer, "q_g")
                if kind == "kr":
                    return slice(64, 96), krb[64:96, 0:w], p_(layer, "kr_g")[64:96, :]
                if kind == "kn":
                    return slice(0, P), kraw[:, j, 0:w], p_(layer, "kn_g")
                return slice(0, C_QK), qC[0:C_QK, j, 0:w], p_(layer, "qc_g")[0:C_QK, :]

            def normalise(layer, t):
                tile = TILES[t]
                g = GROUP_OF.get(tile)
                if g is None or GROUPS[g][0][-1] != tile:
                    return
                gn = group_at[layer, g]
                dve.wait_ge(r_ready, gn)
                dve.wait_ge(raw_done, mm_at[layer, tile])
                rows = {"krope": slice(64, 96), "mla": slice(0, C_QK)}.get(GROUPS[g][1], slice(0, P))
                if roped[0]:
                    dve.wait_ge(rope_done, roped[0])
                refine(rows, gn % 2, nq(layer, tile), SS_BANK(gn), {0: C_KV_RANK, 1: C_Q_RANK}.get(g, 1))
                for name in GROUPS[g][0]:
                    w = nq(layer, name)
                    r = rr[:, gn % 2, 0:w]
                    j = int(name[-1]) if name[-1].isdigit() else 0
                    if name.startswith("kn"):
                        for half in range(2):
                            rows = slice(64 * half, 64 * half + 64)
                            last = dve.tensor_tensor(kC[0:64, 2 * j + half, :], kraw[rows, j, :], r[rows, :], ALU.mult)
                    else:
                        rows, v, _ = kept(layer, name, j, w)
                        last = dve.tensor_tensor(v, v, r[rows, :], ALU.mult)
                last.then_inc(nrm_done, 1)

            def rope(layer, t):
                tile = TILES[t]
                g = GROUP_OF.get(tile)
                if g is None or not GROUPS[g][2]:
                    return
                n = roped_at[layer, g]
                j = int(tile[-1]) if tile[-1].isdigit() else 0
                rows, v, _ = kept(layer, tile, j, NX)
                which = "a" if tile in ("ka",) or tile.startswith("qa") else "c"
                dve.wait_ge(rot_done, n)
                if n > 1:
                    dve.wait_ge(rope_done, n - 1)
                roped[0] = n
                dve.tensor_tensor(tmp[rows, 0, 0:NX], v, c_("cos_" + which)[rows, :], ALU.mult)
                chained(dve.tensor_tensor(tmp[rows, 1, 0:NX], ps[rows, ROT_BANK, 0:NX], c_("sin_" + which)[rows, :],
                                          ALU.mult))
                dve.tensor_tensor(v, tmp[rows, 0, 0:NX], tmp[rows, 1, 0:NX], ALU.add).then_inc(rope_done, 1)
                if tile == "ka":
                    dve.wait_ge(rope_done, n)
                    for kv in range(2):
                        for half in range(2):
                            last = dve.tensor_copy(kA[64 * half:64 * half + 64, kv, :], kraw[64 * kv:64 * kv + 64, 0, :])
                    last.then_inc(spread_done, 1)
                if tile == "kr":
                    dve.wait_ge(rope_done, n)
                    for h in range(C_HEADS):
                        last = dve.tensor_copy(kC[64:96, h, :], krb[64:96, :])
                    last.then_inc(spread_done, 1)

            def conv_taps(layer, count):
                for _ in range(count):
                    n = conv[0]
                    if n >= CONV_STEPS[layer]:
                        return
                    tap, c = divmod(n - 2 * TAPS * layer, 2)
                    s = STREAMS[layer]
                    y = yconv[:, c, 0:s * NX].rearrange("p (s t) -> p s t", s=s)
                    u = upad[:, c, 0:s, tap:tap + NX]
                    wt = p_(layer, "conv_w", c * TAPS + tap)
                    if tap == 0:
                        dve.wait_ge(raw_done, mm_at[layer, "ug1"])
                        ins = dve.tensor_scalar(y, u, wt, p_(layer, "conv_b", c), ALU.mult, ALU.add)
                    else:
                        dve.wait_ge(conv_step, n - 1)
                        ins = dve.scalar_tensor_tensor(out=y, in0=u, scalar=wt, in1=y, op0=ALU.mult, op1=ALU.add)
                    ins.then_inc(conv_step, 1)
                    conv[0] += 1

            def projections(layer):
                for t in range(len(TILES)):
                    keep(layer, t)
                    if t >= 1:
                        normalise(layer, t - 1)
                    if t >= 2:
                        rope(layer, t - 2)
                    if layer == 0 and t - 2 in ADA_AFTER_TILE:
                        ada_store(0, ADA_AFTER_TILE[t - 2])
                    if t >= 4:
                        conv_taps(layer, 4)
                normalise(layer, len(TILES) - 1)
                rope(layer, len(TILES) - 2)
                rope(layer, len(TILES) - 1)
                if layer == 0:
                    ada_store(0, ADA_G - 1)

            def maxima(layer, a):
                kind, pair, stream_, q = attention_units(layer)[a]
                n = att_at[layer, a]
                b = n % 2
                banks = ps[:, 2 * b:2 * b + 2, :]
                dve.wait_ge(s_done, n)
                if kind == "A" and stream_ == 0:
                    lo = P if q == 0 else 0
                    m = c_("mask0" if q == 0 else "mask1")
                    for hh in range(2):
                        last = dve.tensor_tensor(banks[:, hh, lo:lo + P], banks[:, hh, lo:lo + P], m, ALU.add)
                    chained(last)
                chained(dve.tensor_reduce(mx[:, b, :], banks[:, :, 0:T - stream_ * NX], AX.X, ALU.max))
                if kind == "A":
                    ns = nsink[:, layer, 2 * pair:2 * pair + 2]
                    chained(dve.scalar_tensor_tensor(out=nm[:, b, :], in0=mx[:, b, :], scalar=-A_SCALE, in1=ns,
                                                     op0=ALU.mult, op1=ALU.min))
                    dve.tensor_tensor(sm[:, b, :], nm[:, b, :], ns, ALU.subtract).then_inc(max_done, 1)
                else:
                    dve.tensor_scalar(nm[:, b, :], mx[:, b, :], -C_SCALE, None, ALU.mult).then_inc(max_done, 1)

            def shares(layer, a):
                kind, _, stream_, _ = attention_units(layer)[a]
                n = att_at[layer, a]
                b = n % 2
                w = T - stream_ * NX
                dve.wait_ge(exp_done, n)
                total = den[:, b, :]
                if kind == "A":
                    chained(dve.tensor_tensor(dsum[:, :], den[:, b, :], es[:, b, :], ALU.add))
                    total = dsum[:, :]
                chained(dve.reciprocal(rden[:, :], total))
                for hh in range(2):
                    v = probs[:, 2 * b + hh, 0:w]
                    last = dve.tensor_scalar(v, v, rden[:, hh:hh + 1], None, ALU.mult)
                last.then_inc(soft_done, 1)

            def turned(layer, a):
                n = att_at[layer, a]
                w = T - attention_units(layer)[a][2] * NX
                dve.wait_ge(tr_done, n)
                if n > 2:
                    dve.wait_ge(pv_done, n - 2)
                dve.tensor_copy(probs_t[:, 2 * (n % 2) + 1, 0:w], ps[:, 5, 0:w]).then_inc(trc_dve, 1)

            def outputs(layer, a):
                kind, pair, stream_, q = attention_units(layer)[a]
                n = att_at[layer, a]
                q0 = stream_ * NX + q * P
                dve.wait_ge(pv_done, n)
                dve.tensor_copy(hT[:, pair + (6 if kind == "C" else 0), q0:q0 + P], ps[:, 6, 0:P]).then_inc(o_done, 1)

            def attention(layer):
                units = attention_units(layer)
                mean_at, var_at = CONV_AT[layer]
                w = NX * STREAMS[layer]
                maxima(layer, 0)
                for a in range(len(units)):
                    if a + 1 < len(units):
                        maxima(layer, a + 1)
                    shares(layer, a)
                    turned(layer, a)
                    if a >= 1:
                        outputs(layer, a - 1)
                    if a == mean_at + 1:
                        dve.wait_ge(mu_done, layer + 1)
                        for c in range(2):
                            dve.scalar_tensor_tensor(out=yconv[:, c, 0:w], in0=ps[:, 7, 0:w], scalar=-1.0 / B_CH,
                                                     in1=yconv[:, c, 0:w], op0=ALU.mult, op1=ALU.add).then_inc(dev_done, 1)
                    if a == var_at + 2:
                        dve.wait_ge(lnr_ready, layer + 1)
                        refine(slice(0, P), 1, w, 7, B_CH)
                        for c in range(2):
                            y = yconv[:, c, 0:w]
                            chained(dve.scalar_tensor_tensor(out=y, in0=y, scalar=p_(layer, "ln_g", c), in1=rr[:, 1, 0:w],
                                                             op0=ALU.mult, op1=ALU.mult))
                            dve.tensor_scalar(y, y, p_(layer, "ln_b", c), None, ALU.add).then_inc(z_done, 1)
                outputs(layer, len(units) - 1)
                for c in range(2):
                    dve.wait_ge(sig_done, 4 * layer + 3 + c)
                    dve.tensor_tensor(hT[:, 4 + c, 0:w], yconv[:, c, 0:w], tmp[:, c, 0:w], ALU.mult).then_inc(ob_done, 1)

            def residual(which, k, bank):
                layer, chunk = which // 2, (2, 5, 2)[which]
                n = res_at[which, k]
                dve.wait_ge(wo_done, n)
                for s in range(2 if which < 2 else 1):
                    c = slice(s * NX, (s + 1) * NX)
                    last = dve.scalar_tensor_tensor(out=xT[:, k, c], in0=ps[:, bank, c],
                                                    scalar=mod[:, layer, s, chunk * KD + k:chunk * KD + k + 1],
                                                    in1=xT[:, k, c], op0=ALU.mult, op1=ALU.add)
                last.then_inc(res_done, 1)

            def dense():
                for f in range(FT):
                    dve.wait_ge(silu_done, f + 1)
                    dve.tensor_tensor(hid[:, f, :], act_s[:, f % 2, :], ps[:, 2 + f % 2, :], ALU.mult).then_inc(hid_done, 1)
                    if f - 2 in ADA_AFTER_UP:
                        ada_store(1, ADA_AFTER_UP[f - 2])
                for k in range(KD):
                    residual(1, k, 4 + k % 2)

            chained(dve.memset(cact[:, :, :], 0.0))
            dve.wait_ge(small_loaded, 16 * 5)
            dve.wait_ge(act_step, 1)
            dve.tensor_tensor(cact[:, :, 0:2], ccol[:, :, :], csig[:, :, :], ALU.mult).then_inc(cact_ready, 1)
            for layer in range(DEPTH):
                last = dve.tensor_scalar(nsink[:, layer, :], p_(layer, "sink", 0, A_HEADS), -1.0, None, ALU.mult)
            chained(last)
            for g in range(2):
                ada_store(0, g)
            scale_in(0)
            for layer in range(DEPTH):
                chained(dve.memset(upad, 0.0))
                if layer:
                    scale_in(2)
                projections(layer)
                attention(layer)
                for k in range(KD):
                    residual(2 * layer, k, k % 2)
                scale_in(2 * layer + 1)
                if layer == 0:
                    dense()

            U = EXP_U // 3
            for b in range(4):
                dve.memset(yT[:, 2 * b:2 * b + 2, :], 0.0).then_inc(y_done, 1)
            chained(dve.memset(pos, 0.0))
            chained(dve.memset(gate, 0.0))
            chained(dve.memset(g_e, 0.0))
            chained(dve.memset(meta_f, 0.0))
            chained(dve.memset(rtab("one8"), 1.0))
            dve.wait_ge(logit_mm, 1)
            for tt in range(2):
                last = dve.tensor_tensor(rtab("lg")[:, tt, :], ps[:, 0, tt * NE:(tt + 1) * NE], moep[:, KD * NE:KD * NE + NE],
                                         ALU.add)
            chained(last)
            for tt in range(2):
                last = dve.max(rtab("top")[:, tt, :], rtab("lg")[:, tt, :])
            chained(last)
            for tt in range(2):
                last = dve.max_index(idx8[:, tt, :], rtab("top")[:, tt, :], rtab("lg")[:, tt, :])
            chained(last)
            dve.tensor_tensor(rtab("gap"), rtab("top")[:, :, 1], rtab("top")[:, :, 0], ALU.subtract).then_inc(gap_ready, 1)
            chained(dve.tensor_copy(rtab("idx"), idx8[:, :, :]))
            for tt in range(2):
                for which in range(2):
                    last = dve.tensor_scalar(rtab("hot%d" % which)[:, tt, :], c_("eight"),
                                             rtab("idx")[:, tt, which:which + 1], None, ALU.is_equal)
            chained(last)
            dve.tensor_tensor(rtab("mask"), rtab("hot0"), rtab("hot1"), ALU.add).then_inc(mask_ready, 1)
            dve.wait_ge(gap_exp, 1)
            chained(dve.tensor_scalar(rtab("den"), rtab("gap_e"), 1.0, None, ALU.add))
            chained(dve.reciprocal(rtab("w0"), rtab("den")))
            chained(dve.tensor_tensor(rtab("w1"), rtab("gap_e"), rtab("w0"), ALU.mult))
            for tt in range(2):
                last = dve.tensor_scalar(rtab("gates")[:, tt, :], rtab("hot0")[:, tt, :], rtab("w0")[:, tt:tt + 1], None,
                                         ALU.mult)
            chained(last)
            for tt in range(2):
                last = dve.scalar_tensor_tensor(out=rtab("gates")[:, tt, :], in0=rtab("hot1")[:, tt, :],
                                                scalar=rtab("w1")[:, tt:tt + 1], in1=rtab("gates")[:, tt, :],
                                                op0=ALU.mult, op1=ALU.add)
            chained(last)
            for b in range(2):
                dve.wait_ge(htok_mm, b + 1)
                dve.tensor_copy(htok[:, 0, b * 512:(b + 1) * 512], ps[:, 1 + b, :]).then_inc(htok_dve, 1)
            dve.wait_ge(mask_ready, 1)
            dve.wait_ge(count_mm, 1)
            for tt in range(2):
                last = dve.scalar_tensor_tensor(out=rtab("place")[:, tt, :], in0=ps[:, 5, tt * NE:(tt + 1) * NE], scalar=1.0,
                                                in1=rtab("mask")[:, tt, :], op0=ALU.add, op1=ALU.mult)
            dve.tensor_copy(rtab("count"), ps[:, 5, 2 * NE:3 * NE])
            chained(dve.tensor_scalar(rtab("over"), ps[:, 5, 2 * NE:3 * NE], float(P), None, ALU.is_gt))
            dve.tensor_copy(pos[:, :, 0:NE], rtab("place"))
            dve.tensor_copy(gate[:, :, 0:NE], rtab("gates"))
            chained(dve.tensor_tensor_scan(rtab("upto"), rtab("one8"), rtab("over"), 0.0, ALU.mult, ALU.add))
            dve.tensor_scalar(meta_f[:, 0:NE], rtab("count"), 64.0, None, ALU.is_le)
            dve.tensor_scalar(meta_f[:, NI + 3:NI + 4], rtab("upto")[:, NE - 1:NE], float(NE), None, ALU.add)
            dve.tensor_copy(meta_f[:, NI + 4:NI + 5], rtab("upto")[:, NE - 1:NE])
            chained(dve.tensor_tensor(rtab("rank"), rtab("upto"), rtab("over"), ALU.subtract))
            for x in range(3):
                chained(dve.scalar_tensor_tensor(out=rtab("is_x"), in0=rtab("rank"), scalar=float(x), in1=rtab("over"),
                                                 op0=ALU.is_equal, op1=ALU.mult))
                for src, dst in (("place", pos), ("gates", gate)):
                    for tt in range(2):
                        last = dve.tensor_tensor(rtab("pick")[:, tt, :], rtab(src)[:, tt, :], rtab("is_x"), ALU.mult)
                    chained(last)
                    chained(dve.tensor_reduce(dst[:, :, NE + x:NE + x + 1].rearrange("p a b -> p (a b)"), rtab("pick"), AX.X,
                                              ALU.add))
                chained(dve.tensor_scalar(pos[:, :, NE + x], pos[:, :, NE + x], -float(P), None, ALU.add))
                dve.tensor_tensor(rtab("pick")[:, 0, :], rtab("count"), rtab("is_x"), ALU.mult)
                chained(dve.tensor_tensor(rtab("pick")[:, 1, :], c_("eight"), rtab("is_x"), ALU.mult))
                chained(dve.tensor_reduce(rtab("two"), rtab("pick"), AX.X, ALU.add))
                dve.tensor_scalar(meta_f[:, NE + x:NE + x + 1], rtab("two")[:, 0:1], float(P + 64), None, ALU.is_le)
                chained(dve.tensor_copy(meta_f[:, NI + x:NI + x + 1], rtab("two")[:, 1:2]))
            dve.tensor_copy(meta[:, :], meta_f).then_inc(meta_ready, 1)
            dve.wait_ge(meta_ready, 1)

            def pick(i):
                n = dve.value_load(meta[0:1, bass.ds(i, 1)], min_val=0, max_val=1)
                lo, _ = CONST_AT["slots"]
                slots = cst[:, bass.ds(n * P + lo, P)]
                for tt in range(2):
                    dve.tensor_scalar(sel[:, tt, :], slots, pos[:, tt, bass.ds(i, 1)], None, ALU.is_equal)
                    last = dve.tensor_scalar(selg[:, tt, :], slots, pos[:, tt, bass.ds(i, 1)], gate[:, tt, bass.ds(i, 1)],
                                             ALU.is_equal, ALU.mult)
                last.then_inc(sel_ready, 1)

            def expert(i, narrow):
                m = 64 if narrow else P
                for u in range(U):
                    dve.wait_ge(se_done, i * U + (u + 1))
                    if u >= 2:
                        dve.wait_ge(gt_mm, i * U + (u - 1))
                    if narrow:
                        a, b = ps[64:P, u % 2, 0:256], s_e[64:P, u % 2, :]
                    else:
                        a, b = ps[:, u % 2, 256:512], s_e[:, u % 2, :]
                    dve.tensor_tensor(g_e[0:m, u % 2, :], a, b, ALU.mult).then_inc(ge_done, 1)

            pick(0)
            dve.wait_ge(gather_mm, 1)
            dve.tensor_copy(hTe[:, 4:8, :], ps[:, 7, :].rearrange("p (a b) -> p a b", a=4)).then_inc(hte_dve, 1)
            n_items = dve.value_load(meta[0:1, NI + 3:NI + 4], min_val=NE, max_val=ITEMS)
            with dve.Fori(0, n_items) as i:
                dve.wait_ge(selgt_mm, i + 1)
                dve.tensor_copy(selg_t[:, :], ps[:, 3, 0:NX]).then_inc(selgt_done, 1)
                pick(i + 1)
                narrow = dve.value_load(meta[0:1, bass.ds(i, 1)], min_val=0, max_val=1)
                with dve.If(narrow > 0):
                    expert(i, True)
                with dve.Else():
                    expert(i, False)
                dve.wait_ge(acc_mm, i + 1)
                dve.tensor_copy(outE[:, 512:1024], ps[:, 5, :]).then_inc(oute_dve, 1)
                dve.wait_ge(gather_mm, i + 2)
                dve.tensor_copy(hTe[:, 4:8, :], ps[:, 7, :].rearrange("p (a b) -> p a b", a=4)).then_inc(hte_dve, 1)
                for b in range(4):
                    dve.wait_ge(scatter_mm, i * 4 + (b + 1))
                    y = yT[:, 2 * b:2 * b + 2, :]
                    dve.tensor_tensor(y, y, ps[:, b, :].rearrange("p (a c) -> p a c", a=2), ALU.add).then_inc(y_done, 1)
            dve.wait_ge(y_done, n_items * 4 + 4)
            for k in range(KD):
                last = dve.scalar_tensor_tensor(out=yT[:, k, :], in0=yT[:, k, :],
                                                scalar=mod[:, 1, 0, 5 * KD + k:5 * KD + k + 1], in1=xT[:, k, 0:NX],
                                                op0=ALU.mult, op1=ALU.add)
            last.then_inc(final_done, 1)


def constants():
    out = np.zeros((P, CONST_W), np.float32)

    def put(name, a):
        lo, _ = CONST_AT[name]
        a = np.asarray(a, np.float32)
        out[:a.shape[0], lo:lo + a.shape[1]] = a

    ident = np.eye(P)
    put("ident", ident)
    i = np.arange(P)
    put("head", (i[:, None] // HD == i[None, :] // HD) / HD)
    mla = np.zeros((P, P))
    mla[:C_NOPE, :C_NOPE] = 1 / C_NOPE
    mla[C_NOPE:C_QK, C_NOPE:C_QK] = 1 / C_ROPE
    put("mla", mla)
    put("ones", np.ones((P, P)))

    def rotation(lo, dim, m):
        half = dim // 2
        for base in (lo, lo + half):
            for j in range(half // 2):
                m[base + half // 2 + j, base + j] = -1
                m[base + j, base + half // 2 + j] = 1

    rot_a, rot_c = np.zeros((P, P)), np.zeros((P, P))
    rotation(0, HD, rot_a)
    rotation(HD, HD, rot_a)
    rotation(C_NOPE, C_ROPE, rot_c)
    put("rot_a", rot_a)
    put("rot_c", rot_c)
    tok = np.arange(NX)

    def angles(dim):
        a = dim // 2
        inv = (np.float32(1.0) / (np.float32(10000.0) ** (np.arange(0, a, 2, dtype=np.float32) / np.float32(a)))
               ).astype(np.float32)
        ar = (tok // GRID_W).astype(np.float32)[None, :] * inv[:, None]
        ac = (tok % GRID_W).astype(np.float32)[None, :] * inv[:, None]
        return np.concatenate([ar, ar, ac, ac], 0)

    a = angles(HD)
    put("cos_a", np.cos(np.concatenate([a, a], 0)))
    put("sin_a", np.sin(np.concatenate([a, a], 0)))
    a = angles(C_ROPE)
    cos, sin = np.ones((C_QK, NX)), np.zeros((C_QK, NX))
    cos[C_NOPE:], sin[C_NOPE:] = np.cos(a), np.sin(a)
    put("cos_c", cos)
    put("sin_c", sin)
    put("mask0", np.where(P + i[None, :] - i[:, None] > WINDOW, NEG, 0.0))
    put("mask1", np.where(P + i[:, None] - i[None, :] > WINDOW, NEG, 0.0))
    put("before", i[:, None] < i[None, :])
    put("slots", np.broadcast_to(np.concatenate([1 + i, 1 + i % 64])[None, :], (P, 2 * P)))
    put("eight", np.broadcast_to(np.arange(NE)[None, :], (P, NE)))
    put("eps", np.full((P, 1), EPS))
    return out


def by_rows(w, cols):
    k, n = w.shape
    return w.reshape(k // P, P, n // cols, cols).transpose(2, 1, 0, 3).reshape(n // cols, P, -1)


def weight_units(x):
    out = np.zeros((ALL_U, P, UNIT), np.float32)
    for layer in range(DEPTH):
        ada = by_rows(x["ada_w"][layer], 256)
        w_in = x["w_in"][layer]
        tiles = [by_rows(w_in[:, COL0[t]:COL0[t] + (32 if t == "kr" else P)], 32 if t == "kr" else P)[0]
                 for t in TILES[:16]]
        uq = x["c_w_uq"][layer].reshape(3, P, 384)
        ukv = x["c_w_ukv"][layer].reshape(2, P, C_HEADS, 2, C_NOPE).transpose(0, 1, 3, 2, 4).reshape(2, P, 512)
        w_out = by_rows(x["w_out"][layer], P)
        for u in range(ADA_U):
            out[UNIT_AT["ada", layer, u]] = ada[u]
        for u in range(7):
            out[UNIT_AT["in", layer, u]] = np.concatenate([tiles[2 * u], tiles[2 * u + 1]], 1)
        out[UNIT_AT["in", layer, 7]] = np.concatenate([tiles[14], tiles[15], uq[0], uq[1]], 1)
        out[UNIT_AT["in", layer, 8]][:, 0:384 + 1024] = np.concatenate([uq[2], ukv[0], ukv[1]], 1)
        for u in range(OUT_U):
            out[UNIT_AT["out", layer, u]] = np.concatenate([w_out[2 * u], w_out[2 * u + 1]], 1)
    w1, w3 = by_rows(x["dense_w1"][0], P), by_rows(x["dense_w3"][0], P)
    for f in range(UP_U):
        out[UNIT_AT["up", 0, f]] = np.concatenate([w1[f], w3[f]], 1)
    w2 = x["dense_w2"][0].reshape(FT, P, KD, P).transpose(2, 0, 1, 3).reshape(DOWN_U, 16, P, P)
    for u in range(DOWN_U):
        out[UNIT_AT["down", 0, u]] = w2[u].transpose(1, 0, 2).reshape(P, UNIT)
    ex = out[FRONT:].reshape(NE, EXP_U, P, UNIT)
    for e in range(NE):
        ex[e, 0:22:2] = by_rows(x["moe_w1"][0, e], 256)
        ex[e, 1:22:2] = by_rows(x["moe_w3"][0, e], 256)
        ex[e, 22:33] = x["moe_w2"][0, e].reshape(11, 2, P, D).transpose(0, 2, 1, 3).reshape(11, P, UNIT)
    return out


def small_params(x, layer):
    out = np.zeros((P, PAR_W), np.float32)

    def put(name, a):
        lo, _ = PAR_AT[name]
        out[:a.shape[0], lo:lo + a.shape[1]] = a

    def cols(v):
        return v.reshape(-1, P).T

    put("mix_g", cols(x["mix_norm_g"][layer]))
    put("ffn_g", cols(x["ffn_norm_g"][layer]))
    put("ada_b", cols(x["ada_b"][layer]))
    put("q_g", np.tile(x["a_q_norm_g"][layer], 2)[:, None])
    put("k_g", np.tile(x["a_k_norm_g"][layer], 2)[:, None])
    put("cq_g", cols(x["c_q_rank_norm_g"][layer]))
    put("ckv_g", cols(x["c_kv_rank_norm_g"][layer]))
    put("qc_g", np.concatenate([x["c_q_nope_norm_g"][layer], x["c_q_rope_norm_g"][layer]])[:, None])
    put("kn_g", np.tile(x["c_k_nope_norm_g"][layer], 2)[:, None])
    put("kr_g", np.concatenate([np.zeros(64, np.float32), x["c_k_rope_norm_g"][layer]])[:, None])
    put("conv_w", x["b_conv_w"][layer].reshape(TAPS, 2, P).transpose(2, 1, 0).reshape(P, 2 * TAPS))
    put("conv_b", cols(x["b_conv_b"][layer]))
    put("ln_g", cols(x["b_ln_g"][layer]))
    put("ln_b", cols(x["b_ln_b"][layer]))
    put("sink", np.broadcast_to(x["a_sink"][layer][None, :], (P, A_HEADS)))
    return out


def kernel(**inputs):
    from concourse import bacc
    from concourse.bass_utils import run_bass_kernel_spmd

    x = {k: np.asarray(v) for k, v in inputs.items()}
    tokens = np.concatenate([x["x"][0], x["ctx"][0]], 0)
    router = x["moe_router_w"][0].reshape(KD, P, NE).transpose(1, 0, 2).reshape(P, KD * NE)
    arrays = {
        "in_stream": weight_units(x),
        "in_consts": constants(),
        "in_params": np.stack([small_params(x, layer) for layer in range(DEPTH)]),
        "in_moe": np.concatenate([router, np.broadcast_to(x["moe_router_b"][0][None, :], (P, NE))], 1),
        "in_c": np.ascontiguousarray(np.stack([x["c"][0], x["c_ctx"]], 1).reshape(KD, P, 2).transpose(1, 0, 2)),
        "in_x": np.ascontiguousarray(tokens.reshape(T, KD, P).transpose(2, 1, 0)),
    }
    nc = bacc.Bacc("TRN2", target_bir_lowering=False, num_devices=1)
    args = [nc.dram_tensor(n, a.shape, mybir.dt.from_np(a.dtype), kind="ExternalInput").ap() for n, a in arrays.items()]
    out = nc.dram_tensor("out_x", (P, KD, NX), F32, kind="ExternalOutput").ap()
    backbone(nc, *args, out)
    r = run_bass_kernel_spmd(nc, [arrays], core_ids=[0])
    got = r.results[0]["out_x"]
    return np.ascontiguousarray(got.transpose(2, 1, 0)).reshape(1, NX, D)
```

```python
from contextlib import ExitStack

import numpy as np
import concourse.bass as bass
from concourse import mybir

ALU = mybir.AluOpType
ACT = mybir.ActivationFunctionType
AX = mybir.AxisListType
F32 = mybir.dt.float32
I32 = mybir.dt.int32
U32 = mybir.dt.uint32

P = 128
D = 1024
KD = D // P
NX, NC_TOK = 256, 256
T = NX + NC_TOK
DEPTH = 2
GRID_W = 64
HD = 64
A_HEADS, A_KV = 8, 2
B_CH, TAPS = 256, 31
HALO = TAPS // 2
C_HEADS, C_NOPE, C_ROPE, C_V = 4, 64, 32, 64
C_QK = C_NOPE + C_ROPE
C_Q_RANK, C_KV_RANK = 384, 256
FF = 2816
FT = FF // P
NE = 8
EPS = 1e-6
NEG = -1e30
A_SCALE = HD ** -0.5
C_SCALE = C_QK ** -0.5
WINDOW = 128

UNIT = 2048
RING = 11
ADA_U = 6 * D // 256
IN_U, OUT_U = 9, 4
UP_U, DOWN_U = FT, FT * KD // 16
EXP_U = 3 * FF // 256
A_Q0, A_K0, A_V0, U_A0, U_G0, CQ0, CKV0, KR0 = 0, 512, 640, 768, 1024, 1280, 1664, 1920
TILES = ["ua0", "ua1", "ug0", "ug1", "ckv0", "ckv1", "cq0", "cq1", "cq2", "ka", "kn0", "va", "kr",
         "qa0", "qc0", "qa1", "kn1", "qc1", "qa2", "qc2", "qa3", "qc3", "vc0", "vc1"]
IN_AT = {"ua0": (0, 0), "ua1": (0, 1024), "ug0": (1, 0), "ug1": (1, 1024), "ckv0": (2, 0), "ckv1": (2, 1024),
         "cq0": (3, 0), "cq1": (3, 1024), "cq2": (4, 0), "ka": (4, 1024), "va": (5, 1024), "kr": (6, 1152),
         "qa0": (7, 0), "qa1": (7, 1024), "qa2": (8, 0), "qa3": (8, 1024)}
UKV_AT, UQ_AT = (5, 0), (6, 0)
COL0 = {"ua0": U_A0, "ua1": U_A0 + P, "ug0": U_G0, "ug1": U_G0 + P, "ckv0": CKV0, "ckv1": CKV0 + P,
        "cq0": CQ0, "cq1": CQ0 + P, "cq2": CQ0 + 2 * P, "ka": A_K0, "va": A_V0,
        "qa0": A_Q0, "qa1": A_Q0 + P, "qa2": A_Q0 + 2 * P, "qa3": A_Q0 + 3 * P, "kr": KR0}
GROUPS = [(("ckv0", "ckv1"), "rank", False), (("cq0", "cq1", "cq2"), "rank", False), (("ka",), "head", True),
          (("kn0",), "head", False), (("kr",), "krope", True)]
GROUPS += [g for j in range(4) for g in (((f"qa{j}",), "head", True), ((f"qc{j}",), "mla", True))]
GROUPS.insert(GROUPS.index((("qc1",), "mla", True)), (("kn1",), "head", False))
GROUP_OF = {t: g for g, (ts, _, _) in enumerate(GROUPS) for t in ts}
NORMED = [t for t in TILES if t in GROUP_OF]
ROPED = [g for g, (_, _, roped) in enumerate(GROUPS) if roped]
ADA_G = ADA_U // 4
ADA_AFTER_TILE = {(0, 7): (0, 2), (0, 23): (0, 3), (1, 23): (1, 4)}
ADA_IN_ATTENTION = {0: [(0, 4)]}
ADA_AFTER_UP = {10: (1, 1)}
ADA_AFTER_NORM = {1: [(0, 5), (1, 0)], 2: [(1, 2), (1, 3)], 3: [(1, 5)]}


def stream_plan():
    plan = []

    def ada(groups):
        plan.extend(("ada", layer, 4 * g + j) for layer, g in groups for j in range(4))

    def mixer(layer):
        for u in range(IN_U):
            plan.append(("in", layer, u))
            ada([ADA_AFTER_TILE[key] for key in ((layer, 2 * u + 1),) if key in ADA_AFTER_TILE])
        ada([ADA_AFTER_TILE[key] for key in ((layer, len(TILES) - 1),) if key in ADA_AFTER_TILE])
        ada(ADA_IN_ATTENTION.get(layer, []))
        plan.extend(("out", layer, u) for u in range(OUT_U))
        ada(ADA_AFTER_NORM[2 * layer + 1])

    ada([(0, 0), (0, 1)])
    mixer(0)
    for f in range(UP_U):
        plan.append(("up", 0, f))
        ada([ADA_AFTER_UP[g] for g in (f,) if g in ADA_AFTER_UP])
    plan.extend(("down", 0, u) for u in range(DOWN_U))
    ada(ADA_AFTER_NORM[2])
    mixer(1)
    return plan


PLAN = stream_plan()
UNIT_AT = {u: n for n, u in enumerate(PLAN)}
FRONT = len(PLAN)
ALL_U = FRONT + NE * EXP_U



def columns(sizes):
    at, n = {}, 0
    for name, size in sizes:
        at[name] = (n, n + size)
        n += size
    return at, n


CONST_AT, CONST_W = columns([("ident", P), ("ones", P), ("eps", 1), ("head", P), ("mla", P), ("rot_a", P), ("rot_c", P),
                             ("cos_a", NX), ("sin_a", NX), ("cos_c", NX), ("sin_c", NX), ("mask0", P), ("mask1", P),
                             ("before", P), ("slots", 2 * P), ("eight", NE)])
EARLY_W = CONST_AT["eps"][1]
PAR_AT, PAR_W = columns([("mix_g", KD), ("ffn_g", KD), ("ada_b", 6 * KD), ("q_g", 1), ("k_g", 1), ("cq_g", 3),
                         ("ckv_g", 2), ("qc_g", 1), ("kn_g", 1), ("kr_g", 1), ("conv_w", 2 * TAPS), ("conv_b", 2),
                         ("ln_g", 2), ("ln_b", 2), ("sink", A_HEADS)])
MOEP_AT, MOEP_W = columns([("router", KD * NE), ("router_b", NE)])

ITEMS = NE + 3
NI = ITEMS + 1
META_W = 2 * NI + 8


def numbering(keys):
    return {k: n + 1 for n, k in enumerate(keys)}


def attention_units(layer):
    out = []
    for kind, pairs in (("A", 4), ("C", 2)):
        for pair in range(pairs):
            for stream in range(2 if layer == 0 else 1):
                for q in range(2):
                    out.append((kind, pair, stream, q))
    return out


def backbone(nc, stream, consts, params, moe_params, c_cols, x_t, out_t):
    with ExitStack() as ctx:
        def sb(name, shape, dt=F32):
            return ctx.enter_context(nc.sbuf_tensor(name, shape, dt))

        def sem(name):
            return ctx.enter_context(nc.semaphore(name))

        ring = sb("ring", [P, RING, UNIT])
        xT = sb("xT", [P, KD, T])
        hT = sb("hT", [P, KD, T])
        cst = sb("cst", [P, CONST_W])
        par = sb("par", [P, DEPTH, PAR_W])
        moep = sb("moep", [P, MOEP_W])
        ccol = sb("ccol", [P, KD, 2])
        csig = sb("csig", [P, KD, 2])
        cact = sb("cact", [P, KD, 32])
        mod = sb("mod", [P, DEPTH, 2, 6 * KD])
        acol = sb("acol", [P, 4, 2, KD])
        nsink = sb("nsink", [P, DEPTH, A_HEADS])
        adarow = sb("adarow", [P, 256])
        sq = sb("sq", [P, 2, T])
        rr = sb("rr", [P, 2, T])
        tmp = sb("tmp", [P, 2, T])
        rsq = [sb("rsq", [P, T]), tmp[:, 1, :]]
        arena = sb("arena", [P, 14976])

        def carve():
            at = [0]

            def take(*shape):
                n = int(np.prod(shape))
                v = arena[:, at[0]:at[0] + n]
                at[0] += n
                assert at[0] <= 14976, at[0]
                if len(shape) == 2:
                    v = v.rearrange("p (a b) -> p a b", b=shape[1])
                if len(shape) == 3:
                    v = v.rearrange("p (a b c) -> p a b c", b=shape[1], c=shape[2])
                return v
            return take

        take = carve()
        qA, kA = take(4, T), take(2, T)
        vA = take(4, P)
        qC, kC = take(C_HEADS, T), take(C_HEADS, T)
        vC = take(4, C_HEADS * C_V)
        upad = take(2, 2, NX + 2 * HALO)
        yconv = take(2, T)
        pool = take(8, T)
        probs, probs_t = pool[:, 0:4, :], pool[:, 4:8, :]
        kraw = pool[:, 0:2, :]
        cqn, ckvn = pool[:, 2:5, :], pool[:, 5:7, :]
        krb = pool[:, 7, :]
        take = carve()
        hid = take(FT, T)
        act_s = take(2, T)
        take = carve()
        htok = take(2, D)
        hTe = take(KD, P)
        gTe = take(FT, P)
        outE = take(1, D)[:, 0, :]
        sel = take(2, P)
        selg = take(2, P)
        selg_t = take(1, NX)[:, 0, :]
        s_e = take(2, 256)
        g_e = take(2, 256)
        rt = take(1, 512)[:, 0, :]
        pos = take(2, NI)
        rt_at, _ = columns([("lg", 16), ("top", 16), ("idx", 16), ("hot0", 16), ("hot1", 16), ("mask", 16),
                            ("place", 16), ("gates", 16), ("count", 8), ("eight", 8), ("pick", 18 * NE),
                            ("found", 18), ("gap", 2), ("gap_e", 2), ("den", 2), ("w0", 2), ("w1", 2),
                            ("over", 8), ("upto", 8), ("rank", 8), ("is_x", 3 * NE), ("one8", 8)])

        def rtab(name):
            lo, hi = rt_at[name]
            v = rt[:, lo:hi]
            return v.rearrange("p (t e) -> p t e", t=2) if hi - lo == 16 else v

        gate = take(2, NI)
        meta_f = take(1, META_W)[:, 0, :]
        meta = sb("meta", [P, META_W], I32)
        idx8 = sb("idx8", [P, 2, 8], U32)
        mx = sb("mx", [P, 2, 2])
        nm = sb("nm", [P, 2, 2])
        den = sb("den", [P, 2, 2])
        es = sb("es", [P, 2, 2])
        rden = sb("rden", [P, 2])
        sm = sb("sm", [P, 2, 2])
        dsum = sb("dsum", [P, 2])

        ps = ctx.enter_context(nc.psum_tensor("ps", [P, 8, 512], F32))

        def c_(name, a=None, b=None):
            lo, hi = CONST_AT[name]
            return cst[:, lo + (a or 0):hi if b is None else lo + b]

        def p_(layer, name, i=0, n=1):
            lo, _ = PAR_AT[name]
            return par[:, layer, lo + i:lo + i + n]

        slot_loaded = [sem(f"slot_loaded{i}") for i in range(RING)]
        ring_used = sem("ring_used")
        small_loaded, late_loaded, moep_loaded, c_loaded = (sem("small_loaded"), sem("late_loaded"), sem("moep_loaded"),
                                                            sem("c_loaded"))
        x_loaded = sem("x_loaded")
        cact_ready = sem("cact_ready")
        ada_mm, ada_row, ada_tr, ada_mod = sem("ada_mm"), sem("ada_row"), sem("ada_tr"), sem("ada_mod")
        acol_ready = sem("acol_ready")
        sqx_ready, sq_added, ssx_done = sem("sqx_ready"), sem("sq_added"), sem("ssx_done")
        rx_ready, tx_ready, hx_ready = sem("rx_ready"), sem("tx_ready"), sem("hx_ready")
        mm_done, raw_done, sq_done, ss_read = sem("mm_done"), sem("raw_done"), sem("sq_done"), sem("ss_read")
        ln_done, r_ready, nrm_done, rot_done, rope_done = (sem("ln_done"), sem("r_ready"), sem("nrm_done"),
                                                          sem("rot_done"), sem("rope_done"))
        spread_done = sem("spread_done")
        s_done, max_done, exp_done, soft_done = sem("s_done"), sem("max_done"), sem("exp_done"), sem("soft_done")
        tr_done, trc_act, trc_dve, pv_done, o_done = (sem("tr_done"), sem("trc_act"), sem("trc_dve"), sem("pv_done"),
                                                      sem("o_done"))
        conv_step, dve_step, act_step = sem("conv_step"), sem("dve_step"), sem("act_step")
        mu_done, dev_done, dsq_done, var_done, lnr_ready, z_done, sig_done, ob_done = (
            sem("mu_done"), sem("dev_done"), sem("dsq_done"), sem("var_done"), sem("lnr_ready"), sem("z_done"),
            sem("sig_done"), sem("ob_done"))
        wo_done, res_done = sem("wo_done"), sem("res_done")
        up_done, silu_done, hid_done = sem("up_done"), sem("silu_done"), sem("hid_done")
        ge_zero = sem("ge_zero")
        meta_ready, out_stored = sem("meta_ready"), sem("out_stored")
        logit_mm, htok_mm, htok_act, mask_ready, count_mm = (
            sem("logit_mm"), sem("htok_mm"), sem("htok_act"), sem("mask_ready"), sem("count_mm"))
        gap_ready, gap_exp = sem("gap_ready"), sem("gap_exp")
        sel_ready, gather_mm, hte_act, hte_dve = sem("sel_ready"), sem("gather_mm"), sem("hte_act"), sem("hte_dve")
        selgt_mm, selgt_done = sem("selgt_mm"), sem("selgt_done")
        eup_mm, se_done, ge_done, gt_mm, gte_done = (sem("eup_mm"), sem("se_done"), sem("ge_done"), sem("gt_mm"),
                                                    sem("gte_done"))
        acc_mm, oute_act, oute_dve, scatter_mm, y_done = (sem("acc_mm"), sem("oute_act"), sem("oute_dve"),
                                                          sem("scatter_mm"), sem("y_done"))

        def nq(layer, tile):
            keys = tile.startswith(("k", "v", "ckv"))
            return T if layer == 0 or keys else NX

        LT = [(layer, t) for layer in range(DEPTH) for t in TILES]
        mm_at = numbering(LT)
        raw_at = numbering([(layer, t) for layer, t in LT if t not in GROUP_OF])
        normed_at = numbering([(layer, t) for layer in range(DEPTH) for t in NORMED])
        group_at = numbering([(layer, g) for layer in range(DEPTH) for g in range(len(GROUPS))])
        roped_at = numbering([(layer, g) for layer in range(DEPTH) for g in ROPED])
        ada_at = numbering([(layer, g) for layer in range(DEPTH) for g in range(ADA_G)])
        ATT = [(layer, n) for layer in range(DEPTH) for n in range(len(attention_units(layer)))]
        att_at = numbering(ATT)
        STREAMS = [2, 1]
        CONV_AT = [(3, 7), (2, 5)]
        CONV_STEPS = [2 * TAPS, 4 * TAPS]
        NORM_S = [2, 2, 2, 1]
        norm_h_at = numbering([(n, k, s) for n in range(4) for k in range(KD) for s in range(NORM_S[n])])
        norm_sq_at = numbering([(n, k) for n in range(4) for k in range(KD)])
        res_at = numbering([(w, k) for w in range(3) for k in range(KD)])
        MIX_K = [0, 1, 2, 3, 6, 7, 4, 5]
        MAIN_BANK = lambda n: n % 3
        SS_BANK = lambda n: 3 + n % 2
        ROT_BANK, ADA_BANK, ADAT_BANK = 5, 6, 7
        LOGIT_BANKS, HTOK_BANKS = (0, 3), (1, 2, 4, 5)

        def kept(layer, tile, j, w):
            kind = tile.rstrip("0123")
            if kind == "ckv":
                return slice(0, P), ckvn[:, j, 0:w], p_(layer, "ckv_g", j)
            if kind == "cq":
                return slice(0, P), cqn[:, j, 0:w], p_(layer, "cq_g", j)
            if kind == "ka":
                return slice(0, P), kraw[:, 0, 0:w], p_(layer, "k_g")
            if kind == "qa":
                return slice(0, P), qA[:, j, 0:w], p_(layer, "q_g")
            if kind == "kr":
                return slice(64, 96), krb[64:96, 0:w], p_(layer, "kr_g")[64:96, :]
            if kind == "kn":
                return slice(0, P), kraw[:, 1 - j, 0:w], p_(layer, "kn_g")
            return slice(0, C_QK), qC[0:C_QK, j, 0:w], p_(layer, "qc_g")[0:C_QK, :]

        block = ctx.enter_context(nc.Block())

        @block.sync
        def _(sp):
            def unit(n, dst):
                sp.dma_start(ring[:, dst, :], stream[n, :, :]).then_inc(slot_loaded[dst], 16)

            for dst, src in ((cst[:, 0:EARLY_W], consts[:, 0:EARLY_W]), (par[:, 0, :], params[0]), (par[:, 1, :], params[1])):
                sp.dma_start(dst, src).then_inc(small_loaded, 16)
            for k in range(KD):
                sp.dma_start(xT[:, k, :], x_t[:, k, :]).then_inc(x_loaded, 16)
            for s in range(8):
                unit(s, s)
            sp.dma_start(cst[:, EARLY_W:CONST_W], consts[:, EARLY_W:CONST_W]).then_inc(late_loaded, 16)
            for s in range(8, RING):
                unit(s, s)
            sp.dma_start(moep[:, :], moe_params).then_inc(moep_loaded, 16)
            with sp.Fori(1, ALL_U // RING) as r:
                for s in range(RING):
                    sp.wait_ge(ring_used, r * RING + (s + 1 - RING))
                    sp.dma_start(ring[:, s, :], stream[bass.ds(r * RING + s, 1), :, :].rearrange("a p n -> (a p) n")
                                 ).then_inc(slot_loaded[s], 16)
            done = ALL_U // RING * RING
            for n in range(done, ALL_U):
                sp.wait_ge(ring_used, n + 1 - RING)
                unit(n, n % RING)
            sp.wait_ge(meta_ready, 1)
            extra = sp.value_load(meta[0:1, NI + 4:NI + 5], min_val=0, max_val=3)
            with sp.If(extra > 0):
                with sp.Fori(0, extra) as x:
                    expert = sp.value_load(meta[0:1, bass.ds(x + NI, 1)], min_val=0, max_val=NE - 1)
                    for u in range(EXP_U):
                        s = (ALL_U + u) % RING
                        sp.wait_ge(ring_used, x * EXP_U + (ALL_U + u + 1 - RING))
                        sp.dma_start(ring[:, s, :], stream[bass.ds(expert * EXP_U + (FRONT + u), 1), :, :]
                                     .rearrange("a p n -> (a p) n")).then_inc(slot_loaded[s], 16)
            for b in range(4):
                sp.wait_ge(y_done, extra * 4 + (NE * 4 + b + 1))
                sp.dma_start(out_t[:, 2 * b:2 * b + 2, :], xT[:, 2 * b:2 * b + 2, 0:NX]).then_inc(out_stored, 16)
            sp.wait_ge(out_stored, 16 * 4)

        @block.tensor
        def _(pe):
            owed = [0]

            def first(ins):
                if owed[0]:
                    ins.then_inc(ring_used, owed[0])
                    owed[0] = 0

            def arrived(key):
                n = UNIT_AT[key]
                pe.wait_ge(slot_loaded[n % RING], 16 * (n // RING + 1))
                return n % RING

            def ada_rows(layer, g):
                n = ada_at[layer, g]
                slots = [arrived(("ada", layer, 4 * g + j)) for j in range(4)]
                if n > 1:
                    pe.wait_ge(ada_row, n - 1)
                for k in range(KD):
                    for j in range(4):
                        last = pe.matmul(ps[32 * j:32 * j + 32, ADA_BANK, 0:256], cact[:, k, :],
                                         ring[:, slots[j], k * 256:(k + 1) * 256], start=(k == 0), stop=(k == KD - 1))
                        first(last)
                last.then_inc(ada_mm, 1)
                owed[0] += 4

            def ada_turn(layer, g):
                n = ada_at[layer, g]
                pe.wait_ge(ada_row, n)
                if n > 1:
                    pe.wait_ge(ada_mod, n - 1)
                for half in range(2):
                    last = pe.transpose(ps[:, ADAT_BANK, half * P:(half + 1) * P],
                                        adarow[:, half * P:(half + 1) * P], c_("ident"))
                last.then_inc(ada_tr, 1)

            def sum_squares(norm):
                w = NX if norm == 3 else T
                pe.wait_ge(sq_added, (KD - 1) * (norm + 1))
                pe.matmul(ps[:, SS_BANK(0), 0:w], c_("ones"), rr[:, 1, 0:w], start=True, stop=False)
                pe.wait_ge(sqx_ready, norm_sq_at[norm, KD - 1])
                pe.matmul(ps[:, SS_BANK(0), 0:w], c_("ones"), sq[:, (KD - 1) % 2, 0:w], start=False, stop=True
                          ).then_inc(ssx_done, 1)

            def project(layer, t):
                tile = TILES[t]
                n = mm_at[layer, tile]
                bank = MAIN_BANK(n)
                w = nq(layer, tile)
                if n > 3:
                    before = LT[n - 4]
                    if before[1] in GROUP_OF:
                        pe.wait_ge(sq_done, normed_at[before])
                    else:
                        pe.wait_ge(raw_done, raw_at[before])
                if tile in IN_AT:
                    unit_, base = IN_AT[tile]
                    slot = arrived(("in", layer, unit_))
                    wide = 32 if tile == "kr" else P
                    if tile == "va":
                        for q in range(4):
                            for k in range(KD):
                                last = pe.matmul(ps[:, bank, q * P:(q + 1) * P], hT[:, k, q * P:(q + 1) * P],
                                                 ring[:, slot, base + k * P:base + (k + 1) * P],
                                                 start=(k == 0), stop=(k == KD - 1))
                                first(last)
                    else:
                        out = ps[64:96, bank, 0:w] if tile == "kr" else ps[:, bank, 0:w]
                        for k in range(KD):
                            if t == 0:
                                pe.wait_ge(hx_ready, norm_h_at[2 * layer, k, 1])
                            last = pe.matmul(out, ring[:, slot, base + k * wide:base + (k + 1) * wide], hT[:, k, 0:w],
                                             start=(k == 0), stop=(k == KD - 1))
                            first(last)
                    if base == 1024 and unit_ < 5:
                        owed[0] += 1
                elif tile.startswith("qc"):
                    slot, h = arrived(("in", layer, UQ_AT[0])), int(tile[2])
                    pe.wait_ge(nrm_done, group_at[layer, 1])
                    for k in range(3):
                        at = UQ_AT[1] + k * C_HEADS * C_QK + h * C_QK
                        last = pe.matmul(ps[0:C_QK, bank, 0:w], ring[:, slot, at:at + C_QK], cqn[:, k, 0:w],
                                         start=(k == 0), stop=(k == 2))
                        first(last)
                elif tile.startswith("kn"):
                    slot, j = arrived(("in", layer, UKV_AT[0])), int(tile[2])
                    pe.wait_ge(nrm_done, group_at[layer, 0])
                    for k in range(2):
                        at = UKV_AT[1] + k * 512 + j * P
                        last = pe.matmul(ps[:, bank, 0:w], ring[:, slot, at:at + P], ckvn[:, k, 0:w],
                                         start=(k == 0), stop=(k == 1))
                        first(last)
                else:
                    slot, j = arrived(("in", layer, UKV_AT[0])), int(tile[2])
                    for q in range(2):
                        for k in range(2):
                            at = UKV_AT[1] + k * 512 + 256
                            tok = (2 * j + q) * P
                            last = pe.matmul(ps[:, bank, q * 256:(q + 1) * 256], ckvn[:, k, tok:tok + P],
                                             ring[:, slot, at:at + 256], start=(k == 0), stop=(k == 1))
                            first(last)
                last.then_inc(mm_done, 1)
                if t == len(TILES) - 1:
                    owed[0] += IN_U - 5

            def group_sum(layer, t):
                tile = TILES[t]
                if tile not in GROUP_OF:
                    return
                g = GROUP_OF[tile]
                tiles, kind, _ = GROUPS[g]
                gn, n = group_at[layer, g], normed_at[layer, tile]
                w = nq(layer, tile)
                pe.wait_ge(sq_done, n)
                if tile == tiles[0] and gn > 2:
                    pe.wait_ge(nrm_done, gn - 2)
                s = sq[:, n % 2, 0:w]
                kw = dict(start=(tile == tiles[0]), stop=(tile == tiles[-1]))
                if kind == "krope":
                    pe.matmul(ps[64:96, SS_BANK(gn), 0:w], c_("mla", 64, 96)[64:96, :], s[64:96, :], **kw
                              ).then_inc(ss_read, 1)
                elif kind == "mla":
                    pe.matmul(ps[0:C_QK, SS_BANK(gn), 0:w], c_("mla", 0, C_QK)[0:C_QK, :], s[0:C_QK, :], **kw
                              ).then_inc(ss_read, 1)
                else:
                    pe.matmul(ps[:, SS_BANK(gn), 0:w], c_("head" if kind == "head" else "ones"), s, **kw
                              ).then_inc(ss_read, 1)

            def rotate(layer, t):
                tile = TILES[t]
                g = GROUP_OF.get(tile)
                if g is None or not GROUPS[g][2]:
                    return
                n = roped_at[layer, g]
                pe.wait_ge(nrm_done, group_at[layer, g])
                if n > 1:
                    pe.wait_ge(rope_done, n - 1)
                if tile == "kr":
                    pe.matmul(ps[64:96, ROT_BANK, 0:NX], c_("rot_c", 64, 96)[64:96, :], krb[64:96, 0:NX],
                              start=True, stop=True).then_inc(rot_done, 1)
                elif tile.startswith("qc"):
                    pe.matmul(ps[0:C_QK, ROT_BANK, 0:NX], c_("rot_c", 0, C_QK)[0:C_QK, :], qC[0:C_QK, int(tile[2]), 0:NX],
                              start=True, stop=True).then_inc(rot_done, 1)
                else:
                    src = kraw[:, 0, 0:NX] if tile == "ka" else qA[:, int(tile[2]), 0:NX]
                    pe.matmul(ps[:, ROT_BANK, 0:NX], c_("rot_a"), src, start=True, stop=True).then_inc(rot_done, 1)

            def projections(layer):
                for t in range(len(TILES)):
                    project(layer, t)
                    if t >= 1:
                        group_sum(layer, t - 1)
                    if t >= 3:
                        rotate(layer, t - 3)
                    if (layer, t) in ADA_AFTER_TILE:
                        ada_rows(*ADA_AFTER_TILE[layer, t])
                    if (layer, t - 1) in ADA_AFTER_TILE:
                        ada_turn(*ADA_AFTER_TILE[layer, t - 1])
                if (layer, len(TILES) - 1) in ADA_AFTER_TILE:
                    ada_turn(*ADA_AFTER_TILE[layer, len(TILES) - 1])
                rotate(layer, len(TILES) - 3)

            def scores(layer, a):
                kind, pair, stream_, q = attention_units(layer)[a]
                n = att_at[layer, a]
                lo = stream_ * NX
                q0 = lo + q * P
                if n > 2:
                    pe.wait_ge(exp_done, n - 2)
                for hh in range(2):
                    out = ps[:, 2 * (n % 2) + hh, 0:T - lo]
                    if kind == "A":
                        r = slice(64 * hh, 64 * hh + 64)
                        last = pe.matmul(out, qA[r, pair, q0:q0 + P], kA[r, pair // 2, lo:T], start=True, stop=True)
                    else:
                        h = 2 * pair + hh
                        last = pe.matmul(out, qC[0:C_QK, h, q0:q0 + P], kC[0:C_QK, h, lo:T], start=True, stop=True)
                    if hh == 0:
                        first(last)
                last.then_inc(s_done, 1)

            def turn_probs(layer, a):
                _, _, stream_, _ = attention_units(layer)[a]
                n = att_at[layer, a]
                pe.wait_ge(soft_done, n)
                if n > 1:
                    pe.wait_ge(trc_act, n - 1)
                    pe.wait_ge(trc_dve, n - 1)
                for hh in range(2):
                    for b in range(4 - 2 * stream_):
                        last = pe.transpose(ps[:, 4 + hh, b * P:(b + 1) * P],
                                            probs[:, 2 * (n % 2) + hh, b * P:(b + 1) * P], c_("ident"))
                last.then_inc(tr_done, 1)

            def values(layer, a):
                kind, pair, stream_, _ = attention_units(layer)[a]
                n = att_at[layer, a]
                pe.wait_ge(trc_act, n)
                pe.wait_ge(trc_dve, n)
                if n > 1:
                    pe.wait_ge(o_done, n - 1)
                nb = 4 - 2 * stream_
                for b in range(nb):
                    for hh in range(2):
                        kt = b + 2 * stream_
                        if kind == "A":
                            v = vA[:, kt, 64 * (pair // 2):64 * (pair // 2) + 64]
                        else:
                            v = vC[:, kt, 64 * (2 * pair + hh):64 * (2 * pair + hh) + 64]
                        last = pe.matmul(ps[64 * hh:64 * hh + 64, 6, 0:P], v, probs_t[:, 2 * (n % 2) + hh, b * P:(b + 1) * P],
                                         start=(b == 0), stop=(b == nb - 1))
                last.then_inc(pv_done, 1)

            def attention(layer):
                units = attention_units(layer)
                pe.wait_ge(raw_done, raw_at[layer, TILES[-1]])
                pe.wait_ge(nrm_done, group_at[layer, len(GROUPS) - 1])
                pe.wait_ge(rope_done, roped_at[layer, GROUP_OF["qa3"]])
                pe.wait_ge(spread_done, 2 * (layer + 1))
                pe.wait_ge(ada_mod, ada_at[ADA_AFTER_TILE[layer, len(TILES) - 1]])
                scores(layer, 0)
                scores(layer, 1)
                for key in ADA_IN_ATTENTION.get(layer, []):
                    ada_rows(*key)
                mean_at, var_at = CONV_AT[layer]
                pe.wait_ge(rope_done, roped_at[layer, ROPED[-1]])
                for a in range(len(units)):
                    if a + 2 < len(units):
                        scores(layer, a + 2)
                    turn_probs(layer, a)
                    for key in ADA_IN_ATTENTION.get(layer, []) if a == 0 else []:
                        ada_turn(*key)
                    if a == mean_at:
                        for key in ADA_IN_ATTENTION.get(layer, []):
                            pe.wait_ge(ada_mod, ada_at[key])
                    if a >= 1:
                        values(layer, a - 1)
                    w = NX * STREAMS[layer]
                    if a == mean_at:
                        pe.wait_ge(conv_step, CONV_STEPS[layer])
                        for c in range(2):
                            last = pe.matmul(ps[:, 7, 0:w], c_("ones"), yconv[:, c, 0:w], start=(c == 0), stop=(c == 1))
                        last.then_inc(mu_done, 1)
                    if a == var_at:
                        for c in range(2):
                            pe.wait_ge(dsq_done, 2 * layer + c + 1)
                            last = pe.matmul(ps[:, 7, 0:w], c_("ones"), sq[:, c, 0:w], start=(c == 0), stop=(c == 1))
                        last.then_inc(var_done, 1)
                values(layer, len(units) - 1)

            def mixer_out(layer):
                w = NX * STREAMS[layer]
                pe.wait_ge(exp_done, att_at[layer, len(attention_units(layer)) - 1])
                for d in range(KD):
                    slot = arrived(("out", layer, d // 2))
                    n = res_at[2 * layer, d]
                    if d >= 2:
                        pe.wait_ge(res_done, n - 2)
                    for k in MIX_K:
                        if d == 0 and k == MIX_K[4]:
                            pe.wait_ge(o_done, att_at[layer, len(attention_units(layer)) - 1])
                        if d == 0 and k == MIX_K[6]:
                            pe.wait_ge(ob_done, 2 * layer + 2)
                        last = pe.matmul(ps[:, d % 2, 0:w], ring[:, slot, d % 2 * 1024 + k * P:d % 2 * 1024 + (k + 1) * P],
                                         hT[:, k, 0:w], start=(k == MIX_K[0]), stop=(k == MIX_K[-1]))
                        first(last)
                    last.then_inc(wo_done, 1)
                    if d % 2:
                        owed[0] += 1
                sum_squares(2 * layer + 1)
                for key in ADA_AFTER_NORM[2 * layer + 1]:
                    ada_rows(*key)
                    ada_turn(*key)

            def dense():
                for f in range(FT):
                    slot = arrived(("up", 0, f))
                    if f >= 2:
                        pe.wait_ge(hid_done, f - 1)
                    for m in range(2):
                        for k in range(KD):
                            if f == 0 and m == 0:
                                pe.wait_ge(hx_ready, norm_h_at[1, k, 1])
                            last = pe.matmul(ps[:, 2 * m + f % 2, :],
                                             ring[:, slot, m * 1024 + k * P:m * 1024 + (k + 1) * P], hT[:, k, :],
                                             start=(k == 0), stop=(k == KD - 1))
                            first(last)
                    last.then_inc(up_done, 1)
                    owed[0] += 1
                    if f in ADA_AFTER_UP:
                        ada_rows(*ADA_AFTER_UP[f])
                    if f - 1 in ADA_AFTER_UP:
                        ada_turn(*ADA_AFTER_UP[f - 1])
                for d in range(KD):
                    n = res_at[1, d]
                    if d >= 2:
                        pe.wait_ge(res_done, n - 2)
                    for f in range(FT):
                        b = d * FT + f
                        if b % 16 == 0:
                            slot = arrived(("down", 0, b // 16))
                        if d == 0:
                            pe.wait_ge(hid_done, f + 1)
                        last = pe.matmul(ps[:, 4 + d % 2, :], ring[:, slot, b % 16 * P:(b % 16 + 1) * P], hid[:, f, :],
                                         start=(f == 0), stop=(f == FT - 1))
                        if f != FT - 1:
                            first(last)
                        if b % 16 == 15:
                            owed[0] += 1
                    last.then_inc(wo_done, 1)
                sum_squares(2)
                for key in ADA_AFTER_NORM[2]:
                    ada_rows(*key)
                    ada_turn(*key)

            pe.wait_ge(small_loaded, 16 * 3)
            sum_squares(0)
            pe.wait_ge(cact_ready, 1)
            for g in range(2):
                ada_rows(0, g)
                ada_turn(0, g)
            pe.wait_ge(late_loaded, 16)
            projections(0)
            attention(0)
            mixer_out(0)
            dense()
            projections(1)
            attention(1)
            mixer_out(1)
            def unit_wait(u, i):
                n = FRONT + u
                pe.wait_ge(slot_loaded[n % RING], i * (16 * EXP_U // RING) + 16 * (n // RING + 1))
                return n % RING

            def gather():
                for d in range(KD):
                    for tt in range(2):
                        last = pe.matmul(ps[:, 6 + d // 4, d % 4 * P:(d % 4 + 1) * P], htok[:, tt, d * P:(d + 1) * P],
                                         sel[:, tt, :], start=(tt == 0), stop=(tt == 1))
                        first(last)
                last.then_inc(gather_mm, 1)

            U = EXP_U // 3

            def expert(i, narrow):
                for u in range(U + 1):
                    if u < U:
                        b = u % 2
                        if u < 2:
                            pe.wait_ge(y_done, i * 4 + (u + 1))
                        else:
                            pe.wait_ge(ge_done, i * U + (u - 1))
                        if narrow:
                            s1, s3 = unit_wait(2 * u, i), unit_wait(2 * u + 1, i)
                            for k in range(KD):
                                a = pe.matmul(ps[0:64, b, 0:256], hTe[:, k, 0:64], ring[:, s1, k * 256:(k + 1) * 256],
                                              start=(k == 0), stop=(k == KD - 1))
                                first(a)
                                last = pe.matmul(ps[64:P, b, 0:256], hTe[:, k, 0:64], ring[:, s3, k * 256:(k + 1) * 256],
                                                 start=(k == 0), stop=(k == KD - 1))
                        else:
                            for j in range(2):
                                s = unit_wait(2 * u + j, i)
                                for k in range(KD):
                                    last = pe.matmul(ps[:, b, j * 256:(j + 1) * 256], hTe[:, k, :],
                                                     ring[:, s, k * 256:(k + 1) * 256], start=(k == 0), stop=(k == KD - 1))
                                    first(last)
                                if j == 0:
                                    last.then_inc(ring_used, 1)
                        last.then_inc(eup_mm, 1)
                        owed[0] += 2 if narrow else 1
                    if u == 0:
                        pe.wait_ge(y_done, i * 4 + 4)
                        for tt in range(2):
                            last = pe.transpose(ps[:, 3, tt * P:(tt + 1) * P], selg[:, tt, :], c_("ident"))
                        last.then_inc(selgt_mm, 1)
                    else:
                        v = u - 1
                        pe.wait_ge(ge_done, i * U + (v + 1))
                        if v == 0:
                            pe.wait_ge(y_done, i * 4 + 3)
                        elif v == 1:
                            pe.wait_ge(selgt_done, i + 1)
                        else:
                            pe.wait_ge(gte_done, i * U + (v - 1))
                        for half in range(2):
                            last = pe.transpose(ps[:, 2 + v % 2, half * P:(half + 1) * P],
                                                g_e[:, v % 2, half * P:(half + 1) * P], c_("ident"))
                        last.then_inc(gt_mm, 1)
                pe.wait_ge(sel_ready, i + 2)
                gather()
                for u in range(U):
                    s = unit_wait(2 * U + u, i)
                    pe.wait_ge(gte_done, i * U + (u + 1))
                    for n in range(2):
                        for j in range(2):
                            w2 = ring[:, s, j * 1024 + n * 512:j * 1024 + (n + 1) * 512]
                            if narrow:
                                last = pe.matmul(ps[64 * j:64 * j + 64, 4 + n, :], gTe[:, 2 * u + j, 0:64], w2,
                                                 start=(u == 0), stop=(u == U - 1))
                            else:
                                last = pe.matmul(ps[:, 4 + n, :], gTe[:, 2 * u + j, :], w2,
                                                 start=(u == 0 and j == 0), stop=(u == U - 1 and j == 1))
                            if n == 0 and j == 0:
                                first(last)
                    if u < U - 1:
                        last.then_inc(ring_used, 1)
                    else:
                        owed[0] += 1
                last.then_inc(acc_mm, 1)

            pe.wait_ge(moep_loaded, 16)
            for k in range(KD):
                pe.wait_ge(hx_ready, norm_h_at[3, k, 0])
                for tt in range(2):
                    last = pe.matmul(ps[:, LOGIT_BANKS[tt], 0:NE], hT[:, k, tt * P:(tt + 1) * P],
                                     moep[:, k * NE:(k + 1) * NE], start=(k == 0), stop=(k == KD - 1))
                    first(last)
            last.then_inc(logit_mm, 1)
            def turn_tokens(b):
                for k in range(4):
                    last = pe.transpose(ps[:, HTOK_BANKS[b], k * P:(k + 1) * P],
                                        hT[:, b % 2 * 4 + k, b // 2 * P:(b // 2 + 1) * P], c_("ident"))
                last.then_inc(htok_mm, 1)

            turn_tokens(0)
            turn_tokens(1)
            pe.wait_ge(mask_ready, 1)
            for col, parts in ((0, [("before", 0)]), (NE, [("ones", 0), ("before", 1)]),
                               (2 * NE, [("ones", 0), ("ones", 1)])):
                for j, (what, tt) in enumerate(parts):
                    last = pe.matmul(ps[:, 6, col:col + NE], c_(what), rtab("mask")[:, tt, :], start=(j == 0),
                                     stop=(j == len(parts) - 1))
            last.then_inc(count_mm, 1)
            turn_tokens(2)
            turn_tokens(3)
            pe.wait_ge(htok_act, 4)
            pe.wait_ge(sel_ready, 1)
            gather()
            pe.wait_ge(meta_ready, 1)
            n_items = pe.value_load(meta[0:1, NI + 3:NI + 4], min_val=NE, max_val=ITEMS)
            with pe.Fori(0, n_items) as i:
                narrow = pe.value_load(meta[0:1, bass.ds(i, 1)], min_val=0, max_val=1)
                pe.wait_ge(hte_act, i + 1)
                pe.wait_ge(hte_dve, i + 1)
                with pe.If(narrow > 0):
                    expert(i, True)
                owed[0] = 0
                with pe.Else():
                    expert(i, False)
                pe.wait_ge(oute_act, i + 1)
                pe.wait_ge(oute_dve, i + 1)
                for d in range(KD):
                    last = pe.matmul(ps[:, d // 2, d % 2 * NX:(d % 2 + 1) * NX], outE[:, d * P:(d + 1) * P], selg_t[:, :],
                                     start=True, stop=True)
                    if d == 0:
                        first(last)
                    if d % 2:
                        last.then_inc(scatter_mm, 1)

        @block.scalar
        def _(act):
            steps = [0]

            def chained(ins):
                steps[0] += 1
                ins.then_inc(act_step, 1)
                act.wait_ge(act_step, steps[0])

            def squares(norm, k):
                n = norm_sq_at[norm, k]
                if norm == 0:
                    act.wait_ge(x_loaded, 16 * KD)
                else:
                    act.wait_ge(res_done, res_at[norm - 1, k])
                if k >= 2:
                    act.wait_ge(sq_added, (KD - 1) * norm + k - 1)
                elif norm:
                    act.wait_ge(ssx_done, norm)
                w = NX if norm == 3 else T
                act.activation(sq[:, k % 2, 0:w], xT[:, k, 0:w], ACT.Square).then_inc(sqx_ready, 1)

            def root_tables():
                act.preload_act_table_set("natural_log_exp_and_others")

            def norm_root(norm):
                w = NX if norm == 3 else T
                act.wait_ge(ssx_done, norm + 1)
                chained(act.activation(rsq[0][:, 0:w], ps[:, SS_BANK(0), 0:w], ACT.Ln, bias=c_("eps"), scale=1.0 / D))
                chained(act.activation(rr[:, 0, 0:w], rsq[0][:, 0:w], ACT.Exp, scale=-0.5))
                act.activation(rsq[0][:, 0:w], rr[:, 0, 0:w], ACT.Square).then_inc(rx_ready, 1)

            def shift_in(norm):
                layer, chunk = norm // 2, 3 * (norm % 2)
                groups = ADA_AFTER_NORM.get(norm, [])
                if groups:
                    ada_copy(*groups[0])
                for k in range(KD):
                    if k == 3 and len(groups) > 1:
                        ada_copy(*groups[1])
                    for s in range(NORM_S[norm]):
                        n = norm_h_at[norm, k, s]
                        act.wait_ge(tx_ready, n)
                        act.activation(hT[:, k, s * NX:(s + 1) * NX], tmp[:, k % 2, s * NX:(s + 1) * NX], ACT.Identity,
                                       bias=mod[:, layer, s, chunk * KD + k:chunk * KD + k + 1]).then_inc(hx_ready, 1)

            def ada_copy(layer, g):
                n = ada_at[layer, g]
                act.wait_ge(ada_mm, n)
                if n > 1:
                    act.wait_ge(ada_tr, n - 1)
                act.activation(adarow[:, :], ps[:, ADA_BANK, 0:256], ACT.Copy).then_inc(ada_row, 1)

            def tile_squares(layer, t):
                tile = TILES[t]
                w = nq(layer, tile)
                if tile == "ckv0":
                    root_tables()
                if tile.startswith("ug"):
                    act.wait_ge(mm_done, mm_at[layer, tile])
                    act.activation(tmp[:, int(tile[2]), 0:w], ps[:, MAIN_BANK(mm_at[layer, tile]), 0:w], ACT.Sigmoid
                                   ).then_inc(sig_done, 1)
                    return
                if tile not in GROUP_OF:
                    return
                n = normed_at[layer, tile]
                act.wait_ge(mm_done, mm_at[layer, tile])
                if tile == "kn1":
                    act.wait_ge(spread_done, 2 * layer + 1)
                j = int(tile[-1]) if tile[-1].isdigit() else 0
                rows, dst, gain = kept(layer, tile, j, w)
                bank = ps[rows, MAIN_BANK(mm_at[layer, tile]), 0:w]
                act.activation(dst, bank, ACT.Copy, scale=gain)
                if n > 2:
                    act.wait_ge(ss_read, n - 2)
                act.activation(sq[rows, n % 2, 0:w], bank, ACT.Square).then_inc(sq_done, 1)

            def group_root(layer, t):
                tile = TILES[t]
                g = GROUP_OF.get(tile)
                if g is None or GROUPS[g][0][-1] != tile:
                    return
                gn = group_at[layer, g]
                kind = GROUPS[g][1]
                w = nq(layer, tile)
                rows = {"krope": slice(64, 96), "mla": slice(0, C_QK)}.get(kind, slice(0, P))
                scale = {0: 1.0 / C_KV_RANK, 1: 1.0 / C_Q_RANK}.get(g, 1.0)
                act.wait_ge(ss_read, normed_at[layer, tile])
                if gn > 2:
                    act.wait_ge(nrm_done, gn - 2)
                act.activation(rsq[gn % 2][rows, 0:w], ps[rows, SS_BANK(gn), 0:w], ACT.Ln, bias=c_("eps")[rows, :], scale=scale
                               ).then_inc(ln_done, 1)
                act.wait_ge(ln_done, gn)
                chained(act.activation(rr[rows, gn % 2, 0:w], rsq[gn % 2][rows, 0:w], ACT.Exp, scale=-0.5))
                act.activation(rsq[gn % 2][rows, 0:w], rr[rows, gn % 2, 0:w], ACT.Square).then_inc(r_ready, 1)

            def projections(layer):
                for t in range(len(TILES)):
                    tile_squares(layer, t)
                    if t >= 1:
                        group_root(layer, t - 1)
                    if (layer, t - 1) in ADA_AFTER_TILE:
                        ada_copy(*ADA_AFTER_TILE[layer, t - 1])
                if (layer, len(TILES) - 1) in ADA_AFTER_TILE:
                    ada_copy(*ADA_AFTER_TILE[layer, len(TILES) - 1])

            def softmax(layer, a):
                kind, pair, stream_, _ = attention_units(layer)[a]
                n = att_at[layer, a]
                scale = A_SCALE if kind == "A" else C_SCALE
                w = T - stream_ * NX
                act.wait_ge(max_done, n)
                if n > 2:
                    act.wait_ge(tr_done, n - 2)
                for hh in range(2):
                    last = act.activation(probs[:, 2 * (n % 2) + hh, 0:w], ps[:, 2 * (n % 2) + hh, 0:w], ACT.Exp,
                                          bias=nm[:, n % 2, hh:hh + 1], scale=scale, accum_out=den[:, n % 2, hh:hh + 1])
                    if hh == 1 and kind == "C":
                        last.then_inc(exp_done, 1)
                if kind == "A":
                    act.activation(es[:, n % 2, :], sm[:, n % 2, :], ACT.Exp).then_inc(exp_done, 1)

            def turned(layer, a):
                n = att_at[layer, a]
                stream_ = attention_units(layer)[a][2]
                w = T - stream_ * NX
                act.wait_ge(tr_done, n)
                if n > 2:
                    act.wait_ge(pv_done, n - 2)
                act.activation(probs_t[:, 2 * (n % 2), 0:w], ps[:, 4, 0:w], ACT.Copy).then_inc(trc_act, 1)

            def conv_norm(layer):
                w = NX * STREAMS[layer]
                act.wait_ge(var_done, layer + 1)
                chained(act.activation(rsq[1][:, 0:w], ps[:, 7, 0:w], ACT.Ln, bias=c_("eps"), scale=1.0 / B_CH))
                chained(act.activation(rr[:, 1, 0:w], rsq[1][:, 0:w], ACT.Exp, scale=-0.5))
                act.activation(rsq[1][:, 0:w], rr[:, 1, 0:w], ACT.Square).then_inc(lnr_ready, 1)

            def attention(layer):
                units = attention_units(layer)
                mean_at, var_at = CONV_AT[layer]
                w = NX * STREAMS[layer]
                softmax(layer, 0)
                softmax(layer, 1)
                for key in ADA_IN_ATTENTION.get(layer, []):
                    ada_copy(*key)
                for a in range(len(units)):
                    if a == var_at:
                        for c in range(2):
                            act.wait_ge(dev_done, 2 * layer + c + 1)
                            act.activation(sq[:, c, 0:w], yconv[:, c, 0:w], ACT.Square).then_inc(dsq_done, 1)
                    turned(layer, a)
                    if a + 2 < len(units):
                        softmax(layer, a + 2)
                    if a == var_at + 1:
                        conv_norm(layer)
                act.preload_act_table(ACT.Sigmoid)
                for c in range(2):
                    act.wait_ge(z_done, 2 * layer + c + 1)
                    act.activation(tmp[:, c, 0:w], yconv[:, c, 0:w], ACT.Sigmoid).then_inc(sig_done, 1)
                root_tables()

            def dense():
                for f in range(FT):
                    act.wait_ge(up_done, f + 1)
                    if f >= 2:
                        act.wait_ge(hid_done, f - 1)
                    act.activation(act_s[:, f % 2, :], ps[:, f % 2, :], ACT.Silu).then_inc(silu_done, 1)
                    if f - 1 in ADA_AFTER_UP:
                        ada_copy(*ADA_AFTER_UP[f - 1])

            act.dma_start(ccol[:, :, :], c_cols).then_inc(c_loaded, 16)
            act.wait_ge(c_loaded, 16)
            chained(act.activation(csig[:, :, :], ccol[:, :, :], ACT.Sigmoid))
            root_tables()
            for k in range(KD):
                squares(0, k)
            norm_root(0)
            for g in range(2):
                ada_copy(0, g)
            shift_in(0)
            for layer in range(DEPTH):
                if layer:
                    root_tables()
                    for k in range(KD):
                        squares(2, k)
                    norm_root(2)
                    act.preload_act_table(ACT.Sigmoid)
                    shift_in(2)
                projections(layer)
                attention(layer)
                for k in range(KD):
                    squares(2 * layer + 1, k)
                norm_root(2 * layer + 1)
                if layer == 0:
                    act.preload_act_table(ACT.Silu)
                shift_in(2 * layer + 1)
                if layer == 0:
                    dense()
            U = EXP_U // 3

            def expert(i, narrow):
                m = 64 if narrow else P
                for u in range(U + 1):
                    if u < U:
                        act.wait_ge(eup_mm, i * U + (u + 1))
                        if u >= 2:
                            act.wait_ge(ge_done, i * U + (u - 1))
                        dst = s_e[64:P, u % 2, :] if narrow else s_e[:, u % 2, :]
                        act.activation(dst, ps[0:m, u % 2, 0:256], ACT.Silu).then_inc(se_done, 1)
                    if u >= 1:
                        v = u - 1
                        act.wait_ge(gt_mm, i * U + (v + 1))
                        act.activation(gTe[:, 2 * v:2 * v + 2, 0:m],
                                       ps[:, 2 + v % 2, 0:2 * P].rearrange("p (a b) -> p a b", a=2)[:, :, 0:m], ACT.Copy
                                       ).then_inc(gte_done, 1)

            for b in range(4):
                if b == 2:
                    act.wait_ge(gap_ready, 1)
                    act.activation(rtab("gap_e"), rtab("gap"), ACT.Exp).then_inc(gap_exp, 1)
                act.wait_ge(htok_mm, b + 1)
                act.activation(htok[:, b // 2, b % 2 * 512:(b % 2 + 1) * 512], ps[:, HTOK_BANKS[b], :], ACT.Copy
                               ).then_inc(htok_act, 1)
            act.preload_act_table(ACT.Silu)
            act.wait_ge(gather_mm, 1)
            act.activation(hTe[:, 0:4, :], ps[:, 6, :].rearrange("p (a b) -> p a b", a=4), ACT.Copy).then_inc(hte_act, 1)
            act.wait_ge(meta_ready, 1)
            n_items = act.value_load(meta[0:1, NI + 3:NI + 4], min_val=NE, max_val=ITEMS)
            with act.Fori(0, n_items) as i:
                narrow = act.value_load(meta[0:1, bass.ds(i, 1)], min_val=0, max_val=1)
                with act.If(narrow > 0):
                    expert(i, True)
                with act.Else():
                    expert(i, False)
                act.wait_ge(gather_mm, i + 2)
                act.activation(hTe[:, 0:4, :], ps[:, 6, :].rearrange("p (a b) -> p a b", a=4), ACT.Copy
                               ).then_inc(hte_act, 1)
                act.wait_ge(acc_mm, i + 1)
                act.activation(outE[:, 0:512], ps[:, 4, :], ACT.Copy).then_inc(oute_act, 1)

        @block.gpsimd
        def _(gps):
            def add_squares(norm):
                w = NX if norm == 3 else T
                acc = rr[:, 1, 0:w]
                for k in range(KD - 1):
                    gps.wait_ge(sqx_ready, norm_sq_at[norm, k])
                    if k == 0:
                        ins = gps.tensor_copy(acc, sq[:, 0, 0:w])
                    else:
                        gps.wait_ge(sq_added, (KD - 1) * norm + k)
                        ins = gps.tensor_tensor(acc, acc, sq[:, k % 2, 0:w], ALU.add)
                    ins.then_inc(sq_added, 1)

            add_squares(0)
            for layer in range(DEPTH):
                gps.wait_ge(rope_done, roped_at[layer, GROUP_OF["ka"]])
                for kv in range(A_KV):
                    for half in range(2):
                        last = gps.tensor_copy(kA[64 * half:64 * half + 64, kv, :], kraw[64 * kv:64 * kv + 64, 0, :])
                last.then_inc(spread_done, 1)
                gps.wait_ge(rope_done, roped_at[layer, GROUP_OF["kr"]])
                for h in range(C_HEADS):
                    last = gps.tensor_copy(kC[64:96, h, :], krb[64:96, :])
                last.then_inc(spread_done, 1)
                for norm in (1, 2) if layer == 0 else (3,):
                    add_squares(norm)
            gps.wait_ge(rx_ready, 4)
            gps.memset(g_e, 0.0).then_inc(ge_zero, 1)

        @block.vector
        def _(dve):
            steps, conv, roped = [0], [0], [0]

            def chained(ins):
                steps[0] += 1
                ins.then_inc(dve_step, 1)
                dve.wait_ge(dve_step, steps[0])

            def refine(rows, buf, w, bank, count):
                t, root = rsq[buf][rows, 0:w], rr[rows, buf, 0:w]
                chained(dve.scalar_tensor_tensor(out=t, in0=ps[rows, bank, 0:w], scalar=count * EPS, in1=t, op0=ALU.add,
                                                 op1=ALU.mult))
                chained(dve.scalar_tensor_tensor(out=root, in0=t, scalar=-3.0 * count, in1=root, op0=ALU.add,
                                                 op1=ALU.mult))
                return -0.5 / count

            def ada_store(layer, g):
                n = ada_at[layer, g]
                dve.wait_ge(ada_tr, n)
                rows = ps[:, ADAT_BANK, 0:256].rearrange("p (h j s) -> p h j s", h=2, j=4)
                b = p_(layer, "ada_b", KD * g, KD).rearrange("p (j h) -> p h j", h=2)
                for s in range(2):
                    last = dve.tensor_tensor(mod[:, layer, s, KD * g:KD * (g + 1)].rearrange("p (j h) -> p h j", h=2),
                                             rows[:, :, :, s], b, ALU.add)
                last.then_inc(ada_mod, 1)
                if g in (1, 4):
                    norm = 2 * layer + g // 4
                    dve.wait_ge(ada_mod, n)
                    gain = p_(layer, "mix_g" if g == 1 else "ffn_g", 0, KD)
                    for s in range(2):
                        last = dve.scalar_tensor_tensor(out=acol[:, norm, s, :], in0=mod[:, layer, s, KD * g:KD * (g + 1)],
                                                        scalar=1.0, in1=gain, op0=ALU.add, op1=ALU.mult)
                    last.then_inc(acol_ready, 1)

            def scale_in(norm):
                dve.wait_ge(rx_ready, norm + 1)
                w = NX if norm == 3 else T
                factor = refine(slice(0, P), 0, w, SS_BANK(0), D)
                chained(dve.tensor_scalar(rr[:, 0, 0:w], rr[:, 0, 0:w], factor, None, ALU.mult))
                if norm == 0:
                    for g in range(2):
                        ada_store(0, g)
                    dve.wait_ge(late_loaded, 16)
                dve.wait_ge(acol_ready, norm + 1)
                groups = ADA_AFTER_NORM.get(norm, [])
                for k in range(KD):
                    if k == 2 and len(groups) > 1:
                        ada_store(*groups[0])
                    for s in range(NORM_S[norm]):
                        if k >= 2:
                            dve.wait_ge(hx_ready, norm_h_at[norm, k - 2, s])
                        c = slice(s * NX, (s + 1) * NX)
                        dve.scalar_tensor_tensor(out=tmp[:, k % 2, c], in0=xT[:, k, c], scalar=acol[:, norm, s, k:k + 1],
                                                 in1=rr[:, 0, c], op0=ALU.mult, op1=ALU.mult).then_inc(tx_ready, 1)
                if groups:
                    ada_store(*groups[-1])

            def keep(layer, t):
                tile = TILES[t]
                if tile in GROUP_OF:
                    return
                n = mm_at[layer, tile]
                w = nq(layer, tile)
                bank = ps[:, MAIN_BANK(n), :]
                j = int(tile[-1]) if tile[-1].isdigit() else 0
                if tile.startswith("ug"):
                    dve.wait_ge(sig_done, 4 * layer + j + 1)
                    dve.wait_ge(raw_done, raw_at[layer, "ua1"])
                    for s in range(STREAMS[layer]):
                        c = slice(s * NX, (s + 1) * NX)
                        last = dve.tensor_tensor(upad[:, j, s, HALO:HALO + NX], yconv[:, j, c], tmp[:, j, c], ALU.mult)
                    last.then_inc(raw_done, 1)
                    return
                dve.wait_ge(mm_done, n)
                if tile.startswith("ua"):
                    ins = dve.tensor_copy(yconv[:, j, 0:w], bank[:, 0:w])
                elif tile == "va":
                    ins = dve.tensor_copy(vA, bank.rearrange("p (q c) -> p q c", q=4))
                else:
                    ins = dve.tensor_copy(vC[:, 2 * j:2 * j + 2, :], bank.rearrange("p (q c) -> p q c", q=2))
                ins.then_inc(raw_done, 1)

            def normalise(layer, t):
                tile = TILES[t]
                g = GROUP_OF.get(tile)
                if g is None or GROUPS[g][0][-1] != tile:
                    return
                gn = group_at[layer, g]
                dve.wait_ge(r_ready, gn)
                rows = {"krope": slice(64, 96), "mla": slice(0, C_QK)}.get(GROUPS[g][1], slice(0, P))
                factor = refine(rows, gn % 2, nq(layer, tile), SS_BANK(gn), {0: C_KV_RANK, 1: C_Q_RANK}.get(g, 1))
                for name in GROUPS[g][0]:
                    w = nq(layer, name)
                    r = rr[:, gn % 2, 0:w]
                    j = int(name[-1]) if name[-1].isdigit() else 0
                    if name.startswith("kn"):
                        for half in range(2):
                            rows = slice(64 * half, 64 * half + 64)
                            last = dve.scalar_tensor_tensor(out=kC[0:64, 2 * j + half, :], in0=kraw[rows, 1 - j, :],
                                                            scalar=factor, in1=r[rows, :], op0=ALU.mult, op1=ALU.mult)
                    else:
                        rows, v, _ = kept(layer, name, j, w)
                        last = dve.scalar_tensor_tensor(out=v, in0=v, scalar=factor, in1=r[rows, :], op0=ALU.mult,
                                                        op1=ALU.mult)
                last.then_inc(nrm_done, 1)

            def rope(layer, t):
                tile = TILES[t]
                g = GROUP_OF.get(tile)
                if g is None or not GROUPS[g][2]:
                    return
                n = roped_at[layer, g]
                j = int(tile[-1]) if tile[-1].isdigit() else 0
                rows, v, _ = kept(layer, tile, j, NX)
                which = "a" if tile in ("ka",) or tile.startswith("qa") else "c"
                dve.wait_ge(rot_done, n)
                if n > 1:
                    dve.wait_ge(rope_done, n - 1)
                roped[0] = n
                dve.tensor_tensor(tmp[rows, 0, 0:NX], v, c_("cos_" + which)[rows, :], ALU.mult)
                chained(dve.tensor_tensor(tmp[rows, 0, NX:T], ps[rows, ROT_BANK, 0:NX], c_("sin_" + which)[rows, :],
                                          ALU.mult))
                dve.tensor_tensor(v, tmp[rows, 0, 0:NX], tmp[rows, 0, NX:T], ALU.add).then_inc(rope_done, 1)

            def conv_taps(layer, count):
                for _ in range(count):
                    n = conv[0]
                    if n >= CONV_STEPS[layer]:
                        return
                    tap, c = divmod(n - 2 * TAPS * layer, 2)
                    s = STREAMS[layer]
                    y = yconv[:, c, 0:s * NX].rearrange("p (s t) -> p s t", s=s)
                    u = upad[:, c, 0:s, tap:tap + NX]
                    wt = p_(layer, "conv_w", c * TAPS + tap)
                    if tap == 0:
                        dve.wait_ge(raw_done, raw_at[layer, "ug1"])
                        ins = dve.tensor_scalar(y, u, wt, p_(layer, "conv_b", c), ALU.mult, ALU.add)
                    else:
                        dve.wait_ge(conv_step, n - 1)
                        ins = dve.scalar_tensor_tensor(out=y, in0=u, scalar=wt, in1=y, op0=ALU.mult, op1=ALU.add)
                    ins.then_inc(conv_step, 1)
                    conv[0] += 1

            def projections(layer):
                for t in range(len(TILES)):
                    keep(layer, t)
                    if t >= 2:
                        normalise(layer, t - 2)
                    if t >= 3:
                        rope(layer, t - 3)
                    if (layer, t - 2) in ADA_AFTER_TILE:
                        ada_store(*ADA_AFTER_TILE[layer, t - 2])
                    if t >= 4:
                        conv_taps(layer, 6)
                if (layer, len(TILES) - 1) in ADA_AFTER_TILE:
                    ada_store(*ADA_AFTER_TILE[layer, len(TILES) - 1])
                rope(layer, len(TILES) - 3)

            def maxima(layer, a):
                kind, pair, stream_, q = attention_units(layer)[a]
                n = att_at[layer, a]
                b = n % 2
                banks = ps[:, 2 * b:2 * b + 2, :]
                dve.wait_ge(s_done, n)
                if kind == "A" and stream_ == 0:
                    lo = P if q == 0 else 0
                    m = c_("mask0" if q == 0 else "mask1")
                    for hh in range(2):
                        last = dve.tensor_tensor(banks[:, hh, lo:lo + P], banks[:, hh, lo:lo + P], m, ALU.add)
                    chained(last)
                chained(dve.tensor_reduce(mx[:, b, :], banks[:, :, 0:T - stream_ * NX], AX.X, ALU.max))
                if kind == "A":
                    ns = nsink[:, layer, 2 * pair:2 * pair + 2]
                    chained(dve.scalar_tensor_tensor(out=nm[:, b, :], in0=mx[:, b, :], scalar=-A_SCALE, in1=ns,
                                                     op0=ALU.mult, op1=ALU.min))
                    dve.tensor_tensor(sm[:, b, :], nm[:, b, :], ns, ALU.subtract).then_inc(max_done, 1)
                else:
                    dve.tensor_scalar(nm[:, b, :], mx[:, b, :], -C_SCALE, None, ALU.mult).then_inc(max_done, 1)

            def shares(layer, a):
                kind, _, stream_, _ = attention_units(layer)[a]
                n = att_at[layer, a]
                b = n % 2
                w = T - stream_ * NX
                dve.wait_ge(exp_done, n)
                total = den[:, b, :]
                if kind == "A":
                    chained(dve.tensor_tensor(dsum[:, :], den[:, b, :], es[:, b, :], ALU.add))
                    total = dsum[:, :]
                chained(dve.reciprocal(rden[:, :], total))
                for hh in range(2):
                    v = probs[:, 2 * b + hh, 0:w]
                    last = dve.tensor_scalar(v, v, rden[:, hh:hh + 1], None, ALU.mult)
                last.then_inc(soft_done, 1)

            def turned(layer, a):
                n = att_at[layer, a]
                w = T - attention_units(layer)[a][2] * NX
                dve.wait_ge(tr_done, n)
                if n > 2:
                    dve.wait_ge(pv_done, n - 2)
                dve.tensor_copy(probs_t[:, 2 * (n % 2) + 1, 0:w], ps[:, 5, 0:w]).then_inc(trc_dve, 1)

            def outputs(layer, a):
                kind, pair, stream_, q = attention_units(layer)[a]
                n = att_at[layer, a]
                q0 = stream_ * NX + q * P
                dve.wait_ge(pv_done, n)
                dve.tensor_copy(hT[:, pair + (6 if kind == "C" else 0), q0:q0 + P], ps[:, 6, 0:P]).then_inc(o_done, 1)

            def attention(layer):
                units = attention_units(layer)
                mean_at, var_at = CONV_AT[layer]
                w = NX * STREAMS[layer]
                maxima(layer, 0)
                maxima(layer, 1)
                shares(layer, 0)
                for a in range(len(units)):
                    if a + 2 < len(units):
                        maxima(layer, a + 2)
                    turned(layer, a)
                    for key in ADA_IN_ATTENTION.get(layer, []) if a == 0 else []:
                        ada_store(*key)
                    if a + 1 < len(units):
                        shares(layer, a + 1)
                    if a >= 1:
                        outputs(layer, a - 1)
                    if a == mean_at + 1:
                        dve.wait_ge(mu_done, layer + 1)
                        for c in range(2):
                            dve.scalar_tensor_tensor(out=yconv[:, c, 0:w], in0=ps[:, 7, 0:w], scalar=-1.0 / B_CH,
                                                     in1=yconv[:, c, 0:w], op0=ALU.mult, op1=ALU.add).then_inc(dev_done, 1)
                    if a == var_at + 2:
                        dve.wait_ge(lnr_ready, layer + 1)
                        factor = refine(slice(0, P), 1, w, 7, B_CH)
                        chained(dve.tensor_scalar(rr[:, 1, 0:w], rr[:, 1, 0:w], factor, None, ALU.mult))
                        for c in range(2):
                            y = yconv[:, c, 0:w]
                            chained(dve.scalar_tensor_tensor(out=y, in0=y, scalar=p_(layer, "ln_g", c), in1=rr[:, 1, 0:w],
                                                             op0=ALU.mult, op1=ALU.mult))
                            dve.tensor_scalar(y, y, p_(layer, "ln_b", c), None, ALU.add).then_inc(z_done, 1)
                outputs(layer, len(units) - 1)
                for c in range(2):
                    dve.wait_ge(sig_done, 4 * layer + 3 + c)
                    dve.tensor_tensor(hT[:, 4 + c, 0:w], yconv[:, c, 0:w], tmp[:, c, 0:w], ALU.mult).then_inc(ob_done, 1)

            def residual(which, k, bank):
                layer, chunk = which // 2, (2, 5, 2)[which]
                n = res_at[which, k]
                dve.wait_ge(wo_done, n)
                for s in range(2 if which < 2 else 1):
                    c = slice(s * NX, (s + 1) * NX)
                    last = dve.scalar_tensor_tensor(out=xT[:, k, c], in0=ps[:, bank, c],
                                                    scalar=mod[:, layer, s, chunk * KD + k:chunk * KD + k + 1],
                                                    in1=xT[:, k, c], op0=ALU.mult, op1=ALU.add)
                last.then_inc(res_done, 1)

            def dense():
                for f in range(FT):
                    dve.wait_ge(silu_done, f + 1)
                    dve.tensor_tensor(hid[:, f, :], act_s[:, f % 2, :], ps[:, 2 + f % 2, :], ALU.mult).then_inc(hid_done, 1)
                    if f - 2 in ADA_AFTER_UP:
                        ada_store(*ADA_AFTER_UP[f - 2])
                for k in range(KD):
                    residual(1, k, 4 + k % 2)

            chained(dve.memset(cact[:, :, :], 0.0))
            dve.wait_ge(c_loaded, 16)
            dve.wait_ge(act_step, 1)
            dve.tensor_tensor(cact[:, :, 0:2], ccol[:, :, :], csig[:, :, :], ALU.mult).then_inc(cact_ready, 1)
            dve.wait_ge(small_loaded, 16 * 3)
            for layer in range(DEPTH):
                last = dve.tensor_scalar(nsink[:, layer, :], p_(layer, "sink", 0, A_HEADS), -1.0, None, ALU.mult)
            chained(last)
            scale_in(0)
            for layer in range(DEPTH):
                chained(dve.memset(upad, 0.0))
                if layer:
                    scale_in(2)
                projections(layer)
                attention(layer)
                for k in range(KD):
                    residual(2 * layer, k, k % 2)
                scale_in(2 * layer + 1)
                if layer == 0:
                    dense()

            U = EXP_U // 3
            chained(dve.memset(pos, 0.0))
            chained(dve.memset(gate, 0.0))
            chained(dve.memset(meta_f, 0.0))
            chained(dve.memset(rtab("one8"), 1.0))
            dve.wait_ge(logit_mm, 1)
            for tt in range(2):
                last = dve.tensor_tensor(rtab("lg")[:, tt, :], ps[:, LOGIT_BANKS[tt], 0:NE], moep[:, KD * NE:KD * NE + NE],
                                         ALU.add)
            chained(last)
            for tt in range(2):
                last = dve.max(rtab("top")[:, tt, :], rtab("lg")[:, tt, :])
            chained(last)
            for tt in range(2):
                last = dve.max_index(idx8[:, tt, :], rtab("top")[:, tt, :], rtab("lg")[:, tt, :])
            chained(last)
            dve.tensor_tensor(rtab("gap"), rtab("top")[:, :, 1], rtab("top")[:, :, 0], ALU.subtract).then_inc(gap_ready, 1)
            chained(dve.tensor_copy(rtab("idx"), idx8[:, :, :]))
            for tt in range(2):
                for which in range(2):
                    last = dve.tensor_scalar(rtab("hot%d" % which)[:, tt, :], c_("eight"),
                                             rtab("idx")[:, tt, which:which + 1], None, ALU.is_equal)
            chained(last)
            dve.tensor_tensor(rtab("mask"), rtab("hot0"), rtab("hot1"), ALU.add).then_inc(mask_ready, 1)
            dve.wait_ge(gap_exp, 1)
            chained(dve.tensor_scalar(rtab("den"), rtab("gap_e"), 1.0, None, ALU.add))
            chained(dve.reciprocal(rtab("w0"), rtab("den")))
            chained(dve.tensor_tensor(rtab("w1"), rtab("gap_e"), rtab("w0"), ALU.mult))
            for tt in range(2):
                last = dve.tensor_scalar(rtab("gates")[:, tt, :], rtab("hot0")[:, tt, :], rtab("w0")[:, tt:tt + 1], None,
                                         ALU.mult)
            chained(last)
            for tt in range(2):
                last = dve.scalar_tensor_tensor(out=rtab("gates")[:, tt, :], in0=rtab("hot1")[:, tt, :],
                                                scalar=rtab("w1")[:, tt:tt + 1], in1=rtab("gates")[:, tt, :],
                                                op0=ALU.mult, op1=ALU.add)
            chained(last)
            dve.wait_ge(mask_ready, 1)
            dve.wait_ge(count_mm, 1)
            for tt in range(2):
                last = dve.scalar_tensor_tensor(out=rtab("place")[:, tt, :], in0=ps[:, 6, tt * NE:(tt + 1) * NE], scalar=1.0,
                                                in1=rtab("mask")[:, tt, :], op0=ALU.add, op1=ALU.mult)
            dve.tensor_copy(rtab("eight"), c_("eight")).then_inc(y_done, 4)
            dve.tensor_copy(rtab("count"), ps[:, 6, 2 * NE:3 * NE])
            chained(dve.tensor_scalar(rtab("over"), ps[:, 6, 2 * NE:3 * NE], float(P), None, ALU.is_gt))
            dve.tensor_copy(pos[:, :, 0:NE], rtab("place"))
            dve.tensor_copy(gate[:, :, 0:NE], rtab("gates"))
            chained(dve.tensor_tensor_scan(rtab("upto"), rtab("one8"), rtab("over"), 0.0, ALU.mult, ALU.add))
            chained(dve.tensor_scalar(meta_f[:, 0:NE], rtab("count"), 64.0, None, ALU.is_le))
            chained(dve.tensor_copy(meta[:, 0:NE], meta_f[:, 0:NE]))
            def pick(i):
                n = dve.value_load(meta[0:1, bass.ds(i, 1)], min_val=0, max_val=1)
                lo, _ = CONST_AT["slots"]
                slots = cst[:, bass.ds(n * P + lo, P)]
                for tt in range(2):
                    dve.tensor_scalar(sel[:, tt, :], slots, pos[:, tt, bass.ds(i, 1)], None, ALU.is_equal)
                    last = dve.tensor_scalar(selg[:, tt, :], slots, pos[:, tt, bass.ds(i, 1)], gate[:, tt, bass.ds(i, 1)],
                                             ALU.is_equal, ALU.mult)
                last.then_inc(sel_ready, 1)

            def expert(i, narrow):
                m = 64 if narrow else P
                for u in range(U):
                    dve.wait_ge(se_done, i * U + (u + 1))
                    if u >= 2:
                        dve.wait_ge(gt_mm, i * U + (u - 1))
                    if narrow:
                        a, b = ps[64:P, u % 2, 0:256], s_e[64:P, u % 2, :]
                    else:
                        a, b = ps[:, u % 2, 256:512], s_e[:, u % 2, :]
                    dve.tensor_tensor(g_e[0:m, u % 2, :], a, b, ALU.mult).then_inc(ge_done, 1)

            pick(0)
            dve.tensor_scalar(meta_f[:, NI + 3:NI + 4], rtab("upto")[:, NE - 1:NE], float(NE), None, ALU.add)
            dve.tensor_copy(meta_f[:, NI + 4:NI + 5], rtab("upto")[:, NE - 1:NE])
            chained(dve.tensor_tensor(rtab("rank"), rtab("upto"), rtab("over"), ALU.subtract))
            for x in range(3):
                last = dve.scalar_tensor_tensor(out=rtab("is_x")[:, x * NE:(x + 1) * NE], in0=rtab("rank"), scalar=float(x),
                                                in1=rtab("over"), op0=ALU.is_equal, op1=ALU.mult)
            chained(last)
            place_at, pick_at = rt_at["place"][0], rt_at["pick"][0]
            for x in range(3):
                for row in range(6):
                    last = dve.tensor_tensor(rt[:, pick_at + (6 * x + row) * NE:pick_at + (6 * x + row + 1) * NE],
                                             rt[:, place_at + row * NE:place_at + (row + 1) * NE],
                                             rtab("is_x")[:, x * NE:(x + 1) * NE], ALU.mult)
            chained(last)
            chained(dve.tensor_reduce(rtab("found"), rtab("pick").rearrange("p (a b) -> p a b", b=NE), AX.X, ALU.add))
            found = rtab("found").rearrange("p (x r) -> p x r", x=3)
            for tt in range(2):
                dve.tensor_scalar(pos[:, tt, NE:ITEMS], found[:, :, tt], -float(P), None, ALU.add)
                dve.tensor_copy(gate[:, tt, NE:ITEMS], found[:, :, 2 + tt])
            dve.tensor_scalar(meta_f[:, NE:ITEMS], found[:, :, 4], float(P + 64), None, ALU.is_le)
            chained(dve.tensor_copy(meta_f[:, NI:NI + 3], found[:, :, 5]))
            dve.tensor_copy(meta[:, NE:META_W], meta_f[:, NE:META_W]).then_inc(meta_ready, 1)
            dve.wait_ge(meta_ready, 1)
            dve.wait_ge(ge_zero, 1)
            dve.wait_ge(gather_mm, 1)
            dve.tensor_copy(hTe[:, 4:8, :], ps[:, 7, :].rearrange("p (a b) -> p a b", a=4)).then_inc(hte_dve, 1)
            n_items = dve.value_load(meta[0:1, NI + 3:NI + 4], min_val=NE, max_val=ITEMS)
            with dve.Fori(0, n_items) as i:
                dve.wait_ge(selgt_mm, i + 1)
                dve.tensor_copy(selg_t[:, :], ps[:, 3, 0:NX]).then_inc(selgt_done, 1)
                pick(i + 1)
                narrow = dve.value_load(meta[0:1, bass.ds(i, 1)], min_val=0, max_val=1)
                with dve.If(narrow > 0):
                    expert(i, True)
                with dve.Else():
                    expert(i, False)
                dve.wait_ge(gather_mm, i + 2)
                dve.tensor_copy(hTe[:, 4:8, :], ps[:, 7, :].rearrange("p (a b) -> p a b", a=4)).then_inc(hte_dve, 1)
                dve.wait_ge(acc_mm, i + 1)
                dve.tensor_copy(outE[:, 512:1024], ps[:, 5, :]).then_inc(oute_dve, 1)
                for b in range(4):
                    dve.wait_ge(scatter_mm, i * 4 + (b + 1))
                    for k in (2 * b, 2 * b + 1):
                        y = xT[:, k, 0:NX]
                        last = dve.scalar_tensor_tensor(out=y, in0=ps[:, b, k % 2 * NX:(k % 2 + 1) * NX],
                                                        scalar=mod[:, 1, 0, 5 * KD + k:5 * KD + k + 1], in1=y,
                                                        op0=ALU.mult, op1=ALU.add)
                    last.then_inc(y_done, 1)


def constants():
    out = np.zeros((P, CONST_W), np.float32)

    def put(name, a):
        lo, _ = CONST_AT[name]
        a = np.asarray(a, np.float32)
        out[:a.shape[0], lo:lo + a.shape[1]] = a

    ident = np.eye(P)
    put("ident", ident)
    i = np.arange(P)
    put("head", (i[:, None] // HD == i[None, :] // HD) / HD)
    mla = np.zeros((P, P))
    mla[:C_NOPE, :C_NOPE] = 1 / C_NOPE
    mla[C_NOPE:C_QK, C_NOPE:C_QK] = 1 / C_ROPE
    put("mla", mla)
    put("ones", np.ones((P, P)))

    def rotation(lo, dim, m):
        half = dim // 2
        for base in (lo, lo + half):
            for j in range(half // 2):
                m[base + half // 2 + j, base + j] = -1
                m[base + j, base + half // 2 + j] = 1

    rot_a, rot_c = np.zeros((P, P)), np.zeros((P, P))
    rotation(0, HD, rot_a)
    rotation(HD, HD, rot_a)
    rotation(C_NOPE, C_ROPE, rot_c)
    put("rot_a", rot_a)
    put("rot_c", rot_c)
    tok = np.arange(NX)

    def angles(dim):
        a = dim // 2
        inv = (np.float32(1.0) / (np.float32(10000.0) ** (np.arange(0, a, 2, dtype=np.float32) / np.float32(a)))
               ).astype(np.float32)
        ar = (tok // GRID_W).astype(np.float32)[None, :] * inv[:, None]
        ac = (tok % GRID_W).astype(np.float32)[None, :] * inv[:, None]
        return np.concatenate([ar, ar, ac, ac], 0)

    a = angles(HD)
    put("cos_a", np.cos(np.concatenate([a, a], 0)))
    put("sin_a", np.sin(np.concatenate([a, a], 0)))
    a = angles(C_ROPE)
    cos, sin = np.ones((C_QK, NX)), np.zeros((C_QK, NX))
    cos[C_NOPE:], sin[C_NOPE:] = np.cos(a), np.sin(a)
    put("cos_c", cos)
    put("sin_c", sin)
    put("mask0", np.where(P + i[None, :] - i[:, None] > WINDOW, NEG, 0.0))
    put("mask1", np.where(P + i[:, None] - i[None, :] > WINDOW, NEG, 0.0))
    put("before", i[:, None] < i[None, :])
    put("slots", np.broadcast_to(np.concatenate([1 + i, 1 + i % 64])[None, :], (P, 2 * P)))
    put("eight", np.broadcast_to(np.arange(NE)[None, :], (P, NE)))
    put("eps", np.full((P, 1), EPS))
    return out


def by_rows(w, cols):
    k, n = w.shape
    return w.reshape(k // P, P, n // cols, cols).transpose(2, 1, 0, 3).reshape(n // cols, P, -1)


def weight_units(x):
    out = np.zeros((ALL_U, P, UNIT), np.float32)
    for layer in range(DEPTH):
        ada = by_rows(x["ada_w"][layer], 256)
        w_in = x["w_in"][layer]
        for t, (u, at) in IN_AT.items():
            wide = 32 if t == "kr" else P
            out[UNIT_AT["in", layer, u], :, at:at + KD * wide] = by_rows(w_in[:, COL0[t]:COL0[t] + wide], wide)[0]
        uq = x["c_w_uq"][layer].reshape(3, P, 384)
        ukv = x["c_w_ukv"][layer].reshape(2, P, C_HEADS, 2, C_NOPE).transpose(0, 1, 3, 2, 4).reshape(2, P, 512)
        w_out = by_rows(x["w_out"][layer], P)
        for u in range(ADA_U):
            out[UNIT_AT["ada", layer, u]] = ada[u]
        u, at = UQ_AT
        out[UNIT_AT["in", layer, u], :, at:at + 3 * 384] = uq.transpose(1, 0, 2).reshape(P, 3 * 384)
        u, at = UKV_AT
        out[UNIT_AT["in", layer, u], :, at:at + 1024] = ukv.transpose(1, 0, 2).reshape(P, 1024)
        for u in range(OUT_U):
            out[UNIT_AT["out", layer, u]] = np.concatenate([w_out[2 * u], w_out[2 * u + 1]], 1)
    w1, w3 = by_rows(x["dense_w1"][0], P), by_rows(x["dense_w3"][0], P)
    for f in range(UP_U):
        out[UNIT_AT["up", 0, f]] = np.concatenate([w1[f], w3[f]], 1)
    w2 = x["dense_w2"][0].reshape(FT, P, KD, P).transpose(2, 0, 1, 3).reshape(DOWN_U, 16, P, P)
    for u in range(DOWN_U):
        out[UNIT_AT["down", 0, u]] = w2[u].transpose(1, 0, 2).reshape(P, UNIT)
    ex = out[FRONT:].reshape(NE, EXP_U, P, UNIT)
    for e in range(NE):
        ex[e, 0:22:2] = by_rows(x["moe_w1"][0, e], 256)
        ex[e, 1:22:2] = by_rows(x["moe_w3"][0, e], 256)
        ex[e, 22:33] = x["moe_w2"][0, e].reshape(11, 2, P, D).transpose(0, 2, 1, 3).reshape(11, P, UNIT)
    return out


def small_params(x, layer):
    out = np.zeros((P, PAR_W), np.float32)

    def put(name, a):
        lo, _ = PAR_AT[name]
        out[:a.shape[0], lo:lo + a.shape[1]] = a

    def cols(v):
        return v.reshape(-1, P).T

    put("mix_g", cols(x["mix_norm_g"][layer]))
    put("ffn_g", cols(x["ffn_norm_g"][layer]))
    put("ada_b", cols(x["ada_b"][layer]))
    put("q_g", np.tile(x["a_q_norm_g"][layer], 2)[:, None])
    put("k_g", np.tile(x["a_k_norm_g"][layer], 2)[:, None])
    put("cq_g", cols(x["c_q_rank_norm_g"][layer]))
    put("ckv_g", cols(x["c_kv_rank_norm_g"][layer]))
    put("qc_g", np.concatenate([x["c_q_nope_norm_g"][layer], x["c_q_rope_norm_g"][layer]])[:, None])
    put("kn_g", np.tile(x["c_k_nope_norm_g"][layer], 2)[:, None])
    put("kr_g", np.concatenate([np.zeros(64, np.float32), x["c_k_rope_norm_g"][layer]])[:, None])
    put("conv_w", x["b_conv_w"][layer].reshape(TAPS, 2, P).transpose(2, 1, 0).reshape(P, 2 * TAPS))
    put("conv_b", cols(x["b_conv_b"][layer]))
    put("ln_g", cols(x["b_ln_g"][layer]))
    put("ln_b", cols(x["b_ln_b"][layer]))
    put("sink", np.broadcast_to(x["a_sink"][layer][None, :], (P, A_HEADS)))
    return out


def kernel(**inputs):
    from concourse import bacc
    from concourse.bass_utils import run_bass_kernel_spmd

    x = {k: np.asarray(v) for k, v in inputs.items()}
    tokens = np.concatenate([x["x"][0], x["ctx"][0]], 0)
    router = x["moe_router_w"][0].reshape(KD, P, NE).transpose(1, 0, 2).reshape(P, KD * NE)
    arrays = {
        "in_stream": weight_units(x),
        "in_consts": constants(),
        "in_params": np.stack([small_params(x, layer) for layer in range(DEPTH)]),
        "in_moe": np.concatenate([router, np.broadcast_to(x["moe_router_b"][0][None, :], (P, NE))], 1),
        "in_c": np.ascontiguousarray(np.stack([x["c"][0], x["c_ctx"]], 1).reshape(KD, P, 2).transpose(1, 0, 2)),
        "in_x": np.ascontiguousarray(tokens.reshape(T, KD, P).transpose(2, 1, 0)),
    }
    nc = bacc.Bacc("TRN2", target_bir_lowering=False, num_devices=1)
    args = [nc.dram_tensor(n, a.shape, mybir.dt.from_np(a.dtype), kind="ExternalInput").ap() for n, a in arrays.items()]
    out = nc.dram_tensor("out_x", (P, KD, NX), F32, kind="ExternalOutput").ap()
    backbone(nc, *args, out)
    r = run_bass_kernel_spmd(nc, [arrays], core_ids=[0])
    got = r.results[0]["out_x"]
    return np.ascontiguousarray(got.transpose(2, 1, 0)).reshape(1, NX, D)
```
